# Optimizing a Trainium2 kernel written in Bass

```python
import math
import jax, jax.numpy as jnp
from jax import lax
import numpy as np

D_MODEL = 1024
BATCH = 1
SEQ = 512
DEPTH = 2

S5_WIDTH = D_MODEL // 2
S5_GROUP_CH = 16
S5_GROUPS = S5_WIDTH // S5_GROUP_CH
S5_STATE = 64
LRU_WIDTH = D_MODEL // 2
LRU_BLOCKS = 8
LRU_BLOCK_DIM = LRU_WIDTH // LRU_BLOCKS
CONV_WIDTH = 4
RG_C = 8.0
EVEN_IN = S5_WIDTH + 2 * LRU_WIDTH
EVEN_OUT = S5_WIDTH + LRU_WIDTH

MLA_HEADS = 8
Q_LORA = 384
KV_LORA = 256
NOPE_DIM = 128
ROPE_DIM = 64
V_DIM = 128
QK_DIM = NOPE_DIM + ROPE_DIM
MLA_IN = Q_LORA + KV_LORA + ROPE_DIM
ROPE_THETA = 10000.0
Q_BLOCK = 128

N_GROUPS = 8
EXPERTS_PER_GROUP = 8
N_EXPERTS = N_GROUPS * EXPERTS_PER_GROUP
TOP_K = 2
D_EXPERT = 256
MOE_BLOCK = 128

N_EVEN = (DEPTH + 1) // 2
N_ODD = DEPTH // 2
RMS_EPS = 1e-6
NEG_INF = -1e30

kernel_name = "hybrid_s5_rglru_mla_hmoe"

def rms_norm(x, g, eps=RMS_EPS):
    xf = x.astype(jnp.float32)
    y = xf * lax.rsqrt(jnp.mean(xf * xf, axis=-1, keepdims=True) + eps)
    return (y * g.astype(jnp.float32)).astype(x.dtype)

def linear_combine(e1, e2):
    a1, b1 = e1
    a2, b2 = e2
    return (a1 * a2, a2 * b1 + b2)

def complex_linear_combine(e1, e2):
    a1r, a1i, b1r, b1i = e1
    a2r, a2i, b2r, b2i = e2
    return (a2r * a1r - a2i * a1i,
            a2r * a1i + a2i * a1r,
            a2r * b1r - a2i * b1i + b2r,
            a2r * b1i + a2i * b1r + b2i)

def s5_mixer(u, lam_re, lam_im, log_dt, b_re, b_im, c_re, c_im, d, glu_w, glu_b):
    bsz, seq, _ = u.shape
    uf = u.astype(jnp.float32).reshape(bsz, seq, S5_GROUPS, S5_GROUP_CH)
    lr = jnp.minimum(lam_re.astype(jnp.float32), -1e-4)
    li = lam_im.astype(jnp.float32)
    dt = jnp.exp(log_dt.astype(jnp.float32))[:, None]
    mag = jnp.exp(lr * dt)
    lb_re = mag * jnp.cos(li * dt)
    lb_im = mag * jnp.sin(li * dt)
    den = lr * lr + li * li
    num_re = lb_re - 1.0
    f_re = (num_re * lr + lb_im * li) / den
    f_im = (lb_im * lr - num_re * li) / den
    br = b_re.astype(jnp.float32)
    bi = b_im.astype(jnp.float32)
    bbar_re = f_re[..., None] * br - f_im[..., None] * bi
    bbar_im = f_re[..., None] * bi + f_im[..., None] * br
    bu_re = jnp.einsum('blgh,gph->blgp', uf, bbar_re)
    bu_im = jnp.einsum('blgh,gph->blgp', uf, bbar_im)
    a_re = jnp.broadcast_to(lb_re, bu_re.shape)
    a_im = jnp.broadcast_to(lb_im, bu_im.shape)
    _, _, s_re, s_im = lax.associative_scan(
        complex_linear_combine, (a_re, a_im, bu_re, bu_im), axis=1)
    y = (jnp.einsum('blgp,ghp->blgh', s_re, c_re.astype(jnp.float32))
         - jnp.einsum('blgp,ghp->blgh', s_im, c_im.astype(jnp.float32))
         + d.astype(jnp.float32) * uf)
    y = jax.nn.gelu(y.reshape(bsz, seq, S5_WIDTH))
    return y * jax.nn.sigmoid(y @ glu_w.astype(jnp.float32) + glu_b.astype(jnp.float32))

def rglru_mixer(xb, gate_in, conv_w, conv_b, wa, ba, wi, bi, lam):
    bsz, seq, _ = xb.shape
    xc = lax.conv_general_dilated(
        xb, conv_w[:, None, :].astype(xb.dtype), window_strides=(1,),
        padding=[(CONV_WIDTH - 1, 0)], dimension_numbers=('NWC', 'WIO', 'NWC'),
        feature_group_count=LRU_WIDTH)
    xf = xc.astype(jnp.float32) + conv_b.astype(jnp.float32)
    xr = xf.reshape(bsz, seq, LRU_BLOCKS, LRU_BLOCK_DIM)
    r = jax.nn.sigmoid(jnp.einsum('blnc,ncd->blnd', xr, wa.astype(jnp.float32))
                       .reshape(bsz, seq, LRU_WIDTH) + ba.astype(jnp.float32))
    i = jax.nn.sigmoid(jnp.einsum('blnc,ncd->blnd', xr, wi.astype(jnp.float32))
                       .reshape(bsz, seq, LRU_WIDTH) + bi.astype(jnp.float32))
    log_a = RG_C * r * jax.nn.log_sigmoid(lam.astype(jnp.float32))
    a = jnp.exp(log_a)
    b = jnp.sqrt(-jnp.expm1(2.0 * log_a)) * (i * xf)
    _, h = lax.associative_scan(linear_combine, (a, b), axis=1)
    return h * jax.nn.gelu(gate_in.astype(jnp.float32))

def even_mixer(h, w_in, lam_re, lam_im, log_dt, b_re, b_im, c_re, c_im, d, glu_w, glu_b,
               conv_w, conv_b, wa, ba, wi, bi, lam, w_out):
    proj = h @ w_in
    u_s5 = proj[..., :S5_WIDTH]
    x_lru = proj[..., S5_WIDTH:S5_WIDTH + LRU_WIDTH]
    g_lru = proj[..., S5_WIDTH + LRU_WIDTH:]
    ya = s5_mixer(u_s5, lam_re, lam_im, log_dt, b_re, b_im, c_re, c_im, d, glu_w, glu_b)
    yb = rglru_mixer(x_lru, g_lru, conv_w, conv_b, wa, ba, wi, bi, lam)
    y = jnp.concatenate([ya, yb], axis=-1).astype(h.dtype)
    return y @ w_out

def apply_rope(t, cos, sin):
    half = ROPE_DIM // 2
    t1, t2 = t[..., :half], t[..., half:]
    c = cos[:, :, None, :]
    s = sin[:, :, None, :]
    return jnp.concatenate([t1 * c - t2 * s, t1 * s + t2 * c], axis=-1)

def causal_block_attention(q, k, v):
    bsz, seq, nh, dh = q.shape
    dv = v.shape[-1]
    nb = seq // Q_BLOCK
    qb = q.transpose(0, 2, 1, 3).reshape(bsz, nh, nb, Q_BLOCK, dh).transpose(2, 0, 1, 3, 4)
    kt = k.transpose(0, 2, 1, 3)
    vt = v.transpose(0, 2, 1, 3)
    key_pos = jnp.arange(seq)
    scale = 1.0 / math.sqrt(dh)

    def one_block(args):
        q_blk, blk = args
        s = jnp.einsum('bhqd,bhkd->bhqk', q_blk, kt) * scale
        q_pos = blk * Q_BLOCK + jnp.arange(Q_BLOCK)
        s = jnp.where(key_pos[None, :] <= q_pos[:, None], s, NEG_INF)
        p = jax.nn.softmax(s, axis=-1)
        return jnp.einsum('bhqk,bhkd->bhqd', p, vt)

    o = lax.map(one_block, (qb, jnp.arange(nb)))
    return o.transpose(1, 0, 3, 2, 4).reshape(bsz, seq, nh * dv)

def mla_mixer(h, positions, w_in, cq_norm, ckv_norm, w_uq, w_ukv, q_norm, k_norm, w_o):
    bsz, seq, _ = h.shape
    proj = h @ w_in
    c_q = rms_norm(proj[..., :Q_LORA], cq_norm)
    c_kv = rms_norm(proj[..., Q_LORA:Q_LORA + KV_LORA], ckv_norm)
    k_rope = proj[..., Q_LORA + KV_LORA:]
    q = (c_q @ w_uq).reshape(bsz, seq, MLA_HEADS, QK_DIM)
    kv = (c_kv @ w_ukv).reshape(bsz, seq, MLA_HEADS, NOPE_DIM + V_DIM)
    k_nope, v = kv[..., :NOPE_DIM], kv[..., NOPE_DIM:]
    k = jnp.concatenate(
        [k_nope, jnp.broadcast_to(k_rope[:, :, None, :], (bsz, seq, MLA_HEADS, ROPE_DIM))], axis=-1)
    q = rms_norm(q, q_norm).astype(jnp.float32)
    k = rms_norm(k, k_norm).astype(jnp.float32)
    inv_freq = 1.0 / (ROPE_THETA ** (jnp.arange(0, ROPE_DIM, 2, dtype=jnp.float32) / ROPE_DIM))
    ang = positions.astype(jnp.float32)[..., None] * inv_freq
    cos, sin = jnp.cos(ang), jnp.sin(ang)
    q = jnp.concatenate([q[..., :NOPE_DIM], apply_rope(q[..., NOPE_DIM:], cos, sin)], axis=-1)
    k = jnp.concatenate([k[..., :NOPE_DIM], apply_rope(k[..., NOPE_DIM:], cos, sin)], axis=-1)
    o = causal_block_attention(q, k, v.astype(jnp.float32))
    return o.astype(h.dtype) @ w_o

def hierarchical_moe(h, w_group, b_group, w_expert, b_expert, w1, w3, w2):
    bsz, seq, dm = h.shape
    n_tok = bsz * seq
    hf = h.reshape(n_tok, dm)
    g_logits = (hf @ w_group).astype(jnp.float32) + b_group.astype(jnp.float32)
    g_prob = jax.nn.softmax(g_logits, axis=-1)
    g_sel = jnp.argmax(g_logits, axis=-1)
    p_g = jnp.take_along_axis(g_prob, g_sel[:, None], axis=1)[:, 0]
    e_logits = ((hf @ w_expert).astype(jnp.float32) + b_expert.astype(jnp.float32)
                ).reshape(n_tok, N_GROUPS, EXPERTS_PER_GROUP)
    e_in_group = jnp.take_along_axis(e_logits, g_sel[:, None, None], axis=1)[:, 0]
    top_vals, top_idx = lax.top_k(e_in_group, TOP_K)
    gates = p_g[:, None] * jax.nn.softmax(top_vals, axis=-1)
    expert_id = g_sel[:, None].astype(jnp.int32) * EXPERTS_PER_GROUP + top_idx.astype(jnp.int32)
    n_assign = n_tok * TOP_K
    e_flat = expert_id.reshape(-1)
    tok_flat = jnp.arange(n_assign, dtype=jnp.int32) // TOP_K
    g_flat = gates.reshape(-1)
    order = jnp.argsort(e_flat)
    e_sorted = e_flat[order]
    tok_sorted = tok_flat[order]
    g_sorted = g_flat[order]
    counts = jnp.bincount(e_flat, length=N_EXPERTS).astype(jnp.int32)
    starts = jnp.cumsum(counts) - counts
    padded = ((counts + MOE_BLOCK - 1) // MOE_BLOCK) * MOE_BLOCK
    pad_ends = jnp.cumsum(padded)
    pad_starts = pad_ends - padded
    dest = pad_starts[e_sorted] + (jnp.arange(n_assign, dtype=jnp.int32) - starts[e_sorted])
    n_blocks = -(-n_assign // MOE_BLOCK) + N_EXPERTS
    n_rows = n_blocks * MOE_BLOCK
    x_disp = jnp.zeros((n_rows, dm), h.dtype).at[dest].set(hf[tok_sorted])
    blk_start = jnp.arange(n_blocks, dtype=jnp.int32) * MOE_BLOCK
    blk_expert = jnp.clip(jnp.searchsorted(pad_ends, blk_start, side='right'), 0, N_EXPERTS - 1)

    def expert_block(args):
        xb, e = args
        return (jax.nn.silu(xb @ w1[e]) * (xb @ w3[e])) @ w2[e]

    y_disp = lax.map(expert_block, (x_disp.reshape(n_blocks, MOE_BLOCK, dm), blk_expert))
    y_disp = y_disp.reshape(n_rows, dm)
    out = jnp.zeros((n_tok, dm), h.dtype).at[tok_sorted].add(
        g_sorted[:, None].astype(h.dtype) * y_disp[dest])
    return out.reshape(bsz, seq, dm)

def setup_inputs(seed: int = 0) -> dict:
    key = jax.random.key(seed)
    keys = iter(jax.random.split(key, 64))

    def nrm(shape, scale):
        return jax.random.normal(next(keys), shape, jnp.float32) * scale

    def gain(shape):
        return 1.0 + nrm(shape, 0.01)

    x = jax.random.normal(next(keys), (BATCH, SEQ, D_MODEL), jnp.float32)
    offset = jax.random.randint(next(keys), (BATCH, 1), 0, 4096, dtype=jnp.int32)
    positions = offset + jnp.arange(SEQ, dtype=jnp.int32)[None, :]

    n_idx = jnp.arange(S5_STATE, dtype=jnp.float32)
    lam_im0 = jnp.broadcast_to(jnp.pi * n_idx, (N_EVEN, S5_GROUPS, S5_STATE))
    u_lru = jax.random.uniform(next(keys), (N_EVEN, LRU_WIDTH), jnp.float32, 0.9, 0.999)

    return {
        'x': x,
        'positions': positions,
        'ev_norm': gain((N_EVEN, D_MODEL)),
        'ev_w_in': nrm((N_EVEN, D_MODEL, EVEN_IN), D_MODEL ** -0.5),
        's5_lambda_re': -0.5 + nrm((N_EVEN, S5_GROUPS, S5_STATE), 0.01),
        's5_lambda_im': lam_im0 + nrm((N_EVEN, S5_GROUPS, S5_STATE), 0.01),
        's5_log_dt': jax.random.uniform(next(keys), (N_EVEN, S5_GROUPS), jnp.float32,
                                        math.log(1e-3), math.log(1e-1)),
        's5_b_re': nrm((N_EVEN, S5_GROUPS, S5_STATE, S5_GROUP_CH), (2 * S5_GROUP_CH) ** -0.5),
        's5_b_im': nrm((N_EVEN, S5_GROUPS, S5_STATE, S5_GROUP_CH), (2 * S5_GROUP_CH) ** -0.5),
        's5_c_re': nrm((N_EVEN, S5_GROUPS, S5_GROUP_CH, S5_STATE), S5_STATE ** -0.5),
        's5_c_im': nrm((N_EVEN, S5_GROUPS, S5_GROUP_CH, S5_STATE), S5_STATE ** -0.5),
        's5_d': nrm((N_EVEN, S5_GROUPS, S5_GROUP_CH), 1.0),
        's5_glu_w': nrm((N_EVEN, S5_WIDTH, S5_WIDTH), S5_WIDTH ** -0.5),
        's5_glu_b': nrm((N_EVEN, S5_WIDTH), 0.01),
        'lru_conv_w': nrm((N_EVEN, CONV_WIDTH, LRU_WIDTH), CONV_WIDTH ** -0.5),
        'lru_conv_b': nrm((N_EVEN, LRU_WIDTH), 0.01),
        'lru_wa': nrm((N_EVEN, LRU_BLOCKS, LRU_BLOCK_DIM, LRU_BLOCK_DIM), LRU_BLOCK_DIM ** -0.5),
        'lru_ba': nrm((N_EVEN, LRU_WIDTH), 0.01),
        'lru_wi': nrm((N_EVEN, LRU_BLOCKS, LRU_BLOCK_DIM, LRU_BLOCK_DIM), LRU_BLOCK_DIM ** -0.5),
        'lru_bi': nrm((N_EVEN, LRU_WIDTH), 0.01),
        'lru_lambda': jnp.log(u_lru) - jnp.log1p(-u_lru),
        'ev_w_out': nrm((N_EVEN, EVEN_OUT, D_MODEL), EVEN_OUT ** -0.5),
        'od_norm': gain((N_ODD, D_MODEL)),
        'mla_w_in': nrm((N_ODD, D_MODEL, MLA_IN), D_MODEL ** -0.5),
        'mla_cq_norm': gain((N_ODD, Q_LORA)),
        'mla_ckv_norm': gain((N_ODD, KV_LORA)),
        'mla_w_uq': nrm((N_ODD, Q_LORA, MLA_HEADS * QK_DIM), Q_LORA ** -0.5),
        'mla_w_ukv': nrm((N_ODD, KV_LORA, MLA_HEADS * (NOPE_DIM + V_DIM)), KV_LORA ** -0.5),
        'mla_q_norm': gain((N_ODD, QK_DIM)),
        'mla_k_norm': gain((N_ODD, QK_DIM)),
        'mla_w_o': nrm((N_ODD, MLA_HEADS * V_DIM, D_MODEL), (MLA_HEADS * V_DIM) ** -0.5),
        'ffn_norm': gain((DEPTH, D_MODEL)),
        'moe_w_group': nrm((DEPTH, D_MODEL, N_GROUPS), D_MODEL ** -0.5),
        'moe_b_group': nrm((DEPTH, N_GROUPS), 0.01),
        'moe_w_expert': nrm((DEPTH, D_MODEL, N_EXPERTS), D_MODEL ** -0.5),
        'moe_b_expert': nrm((DEPTH, N_EXPERTS), 0.01),
        'moe_w1': nrm((DEPTH, N_EXPERTS, D_MODEL, D_EXPERT), D_MODEL ** -0.5),
        'moe_w3': nrm((DEPTH, N_EXPERTS, D_MODEL, D_EXPERT), D_MODEL ** -0.5),
        'moe_w2': nrm((DEPTH, N_EXPERTS, D_EXPERT, D_MODEL), D_EXPERT ** -0.5),
    }

def reference(x, positions, ev_norm, ev_w_in, s5_lambda_re, s5_lambda_im, s5_log_dt,
              s5_b_re, s5_b_im, s5_c_re, s5_c_im, s5_d, s5_glu_w, s5_glu_b,
              lru_conv_w, lru_conv_b, lru_wa, lru_ba, lru_wi, lru_bi, lru_lambda, ev_w_out,
              od_norm, mla_w_in, mla_cq_norm, mla_ckv_norm, mla_w_uq, mla_w_ukv,
              mla_q_norm, mla_k_norm, mla_w_o,
              ffn_norm, moe_w_group, moe_b_group, moe_w_expert, moe_b_expert,
              moe_w1, moe_w3, moe_w2):
    for layer in range(DEPTH):
        j = layer // 2
        if layer % 2 == 0:
            x = x + even_mixer(
                rms_norm(x, ev_norm[j]), ev_w_in[j], s5_lambda_re[j], s5_lambda_im[j],
                s5_log_dt[j], s5_b_re[j], s5_b_im[j], s5_c_re[j], s5_c_im[j], s5_d[j],
                s5_glu_w[j], s5_glu_b[j], lru_conv_w[j], lru_conv_b[j], lru_wa[j], lru_ba[j],
                lru_wi[j], lru_bi[j], lru_lambda[j], ev_w_out[j])
        else:
            x = x + mla_mixer(
                rms_norm(x, od_norm[j]), positions, mla_w_in[j], mla_cq_norm[j],
                mla_ckv_norm[j], mla_w_uq[j], mla_w_ukv[j], mla_q_norm[j], mla_k_norm[j],
                mla_w_o[j])
        x = x + hierarchical_moe(
            rms_norm(x, ffn_norm[layer]), moe_w_group[layer], moe_b_group[layer],
            moe_w_expert[layer], moe_b_expert[layer], moe_w1[layer], moe_w3[layer],
            moe_w2[layer])
    return x


_drawn_inputs = setup_inputs


def setup_inputs(seed=0):
    import zlib

    import numpy as np

    out = dict(_drawn_inputs(seed))
    spreads = {}
    factors = {'ev_norm': 3.163,
     's5_lambda_re': 8.0,
     's5_glu_b': 8.0,
     'lru_ba': 6.482,
     'lru_bi': 8.0,
     'od_norm': 8.0,
     'mla_cq_norm': 8.0,
     'mla_ckv_norm': 6.906,
     'mla_q_norm': 7.871,
     'mla_k_norm': 8.0,
     'moe_b_expert': 3.334}
    for name, (base, spread) in spreads.items():
        noise = np.random.default_rng([zlib.crc32(name.encode()), seed]).standard_normal(out[name].shape)
        drawn = base * np.exp(spread * noise) if base else spread * noise
        out[name] = __import__('jax').numpy.asarray(drawn.astype(out[name].dtype))
    for name, factor in factors.items():
        out[name] = (out[name] * factor).astype(out[name].dtype)
    return out
```

```python
import math
import concourse.bass as bass
from concourse import mybir
from contextlib import ExitStack
import numpy as np

F32 = mybir.dt.float32
I32 = mybir.dt.int32
ALU = mybir.AluOpType
ACT = mybir.ActivationFunctionType
AX = mybir.AxisListType

P = 128
D = 1024
T = 512
TC = T // P
KC = D // P
W5 = 512
MT = W5 // P
NS5 = 16
H = 8
QL, KVL, NOPE, ROPE, VD = 384, 256, 128, 64, 128
QK = NOPE + ROPE
MLA_IN = QL + KVL + ROPE
ATT_SCALE = 1.0 / math.sqrt(QK)
NG, EG = 8, 8
NE = NG * EG
DE = 256
FC = DE // P
CAP = 64
OVMAX = 2 * T // CAP - 1
NBLK = NE + OVMAX + 1
EPS = 1e-6
ROUND = 12582912.0
TWO_PI = 2.0 * math.pi
PI_1 = 6.28125
PI_2 = float(np.float32(np.round((TWO_PI - PI_1) * 2.0 ** 22) / 2.0 ** 22))
PI_3 = TWO_PI - PI_1 - PI_2
RING = 4

C_ID, C_UP, C_ONE, C_ID2, C_MASK = 0, 128, 256, 384, 448
C_T, C_E, C_I, C_DESC, C_INVF = 576, 1088, 1152, 1168, 1176
C_END = 1208


def shape_constants():
    c = np.zeros((P, C_END), np.float32)
    r = np.arange(P)
    c[:, C_ID:C_ID + P] = np.eye(P)
    c[:, C_UP:C_UP + P] = r[:, None] < r[None, :]
    c[:, C_ONE:C_ONE + P] = 1.0
    c[:, C_ID2:C_ID2 + CAP] = np.eye(CAP)[r % CAP]
    c[:, C_MASK:C_MASK + P] = np.where(r[None, :] <= r[:, None], 0.0, -1e30)
    c[:, C_T:C_T + T] = np.arange(T)
    c[:, C_E:C_E + NE] = np.arange(NE) * CAP
    c[:, C_I:C_I + 16] = np.arange(16)
    c[:, C_DESC:C_DESC + 8] = 8 - np.arange(8)
    c[:, C_INVF:C_INVF + ROPE // 2] = np.float32(1.0) / np.power(
        np.float32(10000.0), np.arange(0, ROPE, 2, dtype=np.float32) / np.float32(ROPE), dtype=np.float32)
    return c


def hybrid_decoder(nc, a, out):
    ctx = ExitStack()
    with ctx:
        def sb(name, shape, dt=F32):
            return ctx.enter_context(nc.sbuf_tensor(name, shape, dt))

        def sem(name):
            return ctx.enter_context(nc.semaphore(name))

        ring = [sb(f"ring{b}", [P, 3, KC * DE]) for b in range(RING)]
        x = sb("x", [P, TC, D])
        rega = sb("region_a", [P, TC * D])
        regb = sb("region_b", [P, KC * T])
        wbuf = sb("wbuf", [P, 2 * KC * 512])
        gain = sb("gain", [P, D])
        con = sb("con", [P, C_END])
        extra = sb("extra", [P, 4096])
        smalls = sb("smalls", [P, 760])
        idx = sb("idx", [P, 8], I32)
        ovi = sb("ovi", [P, 16], I32)
        ps = ctx.enter_context(nc.psum_tensor("ps", [P, 8, 512], F32))

        ident = con[:, C_ID:C_ID + P]
        tri = con[:, C_UP:C_UP + P]
        ones = con[:, C_ONE:C_ONE + P]
        id2 = con[:, C_ID2:C_ID2 + CAP]
        mask = con[:, C_MASK:C_MASK + P]
        tcount = con[:, C_T:C_T + T]

        spot = [0]

        def small(n):
            s = smalls[:, spot[0]:spot[0] + n]
            spot[0] += n
            assert spot[0] <= 760
            return s

        eps = small(1)
        halfpi = small(1)
        ssq, root, rstd = small(4), small(4), small(4)

        h = rega[:, :].rearrange("p (c d) -> p c d", c=TC)
        hT = regb[:, :].rearrange("p (k t) -> p k t", k=KC)
        r2 = ring[2][:, :, :].rearrange("p a b -> p (a b)")
        r3 = ring[3][:, :, :].rearrange("p a b -> p (a b)")
        r1 = ring[1][:, :, :].rearrange("p a b -> p (a b)")

        xdisp = nc.dram_tensor("xdisp", [NBLK * CAP, D], F32, kind="Internal").ap()
        ydisp = nc.dram_tensor("ydisp", [NBLK * CAP, D], F32, kind="Internal").ap()

        s_x, s_con, s_par = sem("s_x"), sem("s_con"), sem("s_par")
        s_gain = sem("s_gain")
        s_ssq, s_root = sem("s_ssq"), sem("s_root")
        s_h = sem("s_h")
        s_tr = sem("s_tr")
        s_eva, s_evv = sem("s_eva"), sem("s_evv")
        s_eps = sem("s_eps")
        s_bar = sem("s_bar")
        s_v = sem("s_v")
        s_g = sem("s_g")
        s_a = sem("s_a")
        s_zero, s_xz = sem("s_zero"), sem("s_xz")
        s_wb = [sem("s_wb0"), sem("s_wb1"), sem("s_wb2"), sem("s_wb3")]
        s_out = sem("s_out")

        chain = {"v": 0, "g": 0, "a": 0}

        def vlink(ins):
            chain["v"] += 1
            ins.then_inc(s_v, 1)
            nc.vector.wait_ge(s_v, chain["v"])

        def glink(ins):
            chain["g"] += 1
            ins.then_inc(s_g, 1)
            nc.gpsimd.wait_ge(s_g, chain["g"])

        def alink(ins):
            chain["a"] += 1
            ins.then_inc(s_a, 1)
            nc.scalar.wait_ge(s_a, chain["a"])

        def barrier(eng, n):
            eng.drain().then_inc(s_bar, 1)
            eng.wait_ge(s_bar, 4 * n)

        V, S, G, TE = nc.vector, nc.scalar, nc.gpsimd, nc.tensor

        def norm_scalar(n):
            for c in range(TC):
                S.activation(h[:, c, :], x[:, c, :], ACT.Square, accum_out=ssq[:, c:c + 1]).then_inc(s_ssq, 1)
            S.wait_ge(s_ssq, TC * (n + 1))
            S.activation(root, ssq, ACT.Sqrt, bias=eps, scale=1.0 / D).then_inc(s_root, 1)
            for c in range(TC):
                S.wait_ge(s_tr, TC * n + c + 1)
                S.activation(hT[:, 0:4, c * P:(c + 1) * P],
                             ps[:, 2 * c, :].rearrange("p (k t) -> p k t", k=4), ACT.Copy).then_inc(s_eva, 1)

        def norm_vector(n):
            V.wait_ge(s_root, n + 1)
            vlink(V.reciprocal(rstd, root))
            V.wait_ge(s_gain, 16 * (n + 1))
            for c in range(TC):
                V.scalar_tensor_tensor(h[:, c, :], x[:, c, :], rstd[:, c:c + 1], gain[:, :],
                                       ALU.mult, ALU.mult).then_inc(s_h, 1)
            for c in range(TC):
                V.wait_ge(s_tr, TC * n + c + 1)
                V.tensor_copy(hT[:, 4:8, c * P:(c + 1) * P],
                              ps[:, 2 * c + 1, :].rearrange("p (k t) -> p k t", k=4)).then_inc(s_evv, 1)

        def norm_tensor(n):
            for c in range(TC):
                TE.wait_ge(s_h, TC * n + c + 1)
                hs = h[:, c, :].rearrange("p (q k) -> p k q", k=KC)
                for k in range(KC):
                    last = TE.transpose(ps[:, 2 * c + k // 4, (k % 4) * P:(k % 4 + 1) * P], hs[:, k, :], ident)
                last.then_inc(s_tr, 1)
            TE.wait_ge(s_eva, TC * (n + 1))
            TE.wait_ge(s_evv, TC * (n + 1))

        uT = r2[:, 0:2048].rearrange("p (m t) -> p m t", m=MT)
        gT = r2[:, 2048:4096].rearrange("p (m t) -> p m t", m=MT)
        rT = r2[:, 4096:6144].rearrange("p (m t) -> p m t", m=MT)
        iT = r3[:, 0:2048].rearrange("p (m t) -> p m t", m=MT)
        XW = T + 3
        xT = r3[:, 2048:2048 + MT * XW].rearrange("p (m t) -> p m t", m=MT)
        cmat = r3[:, 4108:5132].rearrange("p (a s h) -> p a s h", a=2, s=NS5)
        lruw = r3[:, 5132:5644].rearrange("p (a m n) -> p a m n", a=2, m=MT)
        bT = gain[:, :].rearrange("p (a q n) -> p a q n", a=2, q=MT)
        xfT = [extra[:, m * T:(m + 1) * T] for m in range(MT)]
        yl = rega[:, 2048:4096].rearrange("p (m t) -> p m t", m=MT)
        yg = rega[:, 0:2048].rearrange("p (m t) -> p m t", m=MT)
        glu = extra[:, 2048:4096].rearrange("p (k n) -> p k n", k=MT)
        tabc = [regb[:, i * T:(i + 1) * T] for i in range(2)]
        tabs = [regb[:, (2 + i) * T:(3 + i) * T] for i in range(2)]
        ph = [regb[:, (4 + i) * T:(5 + i) * T] for i in range(2)]
        sa = [regb[:, (6 + i) * T:(7 + i) * T] for i in range(2)]
        LR = [r2[:, 4096 + i * T:4096 + (i + 1) * T] for i in range(4)] + [r3[:, i * T:(i + 1) * T] for i in range(8)]
        sbb, pa, pb, pc, pd = LR[0], LR[1], LR[2], LR[3], LR[4]
        zr, zi = pa, pc
        zre, zim = [LR[5], LR[6]], [LR[7], LR[8]]
        ga, gb, gc, gd = [rega[:, i * T:(i + 1) * T] for i in range(4)]
        sre = [LR[9], xfT[0]]
        sim = [xfT[1], xfT[2]]
        tk = xfT[3]

        s5p = small(16 * 3)
        lam_re, lam_im, ldt = s5p[:, 0:16], s5p[:, 16:32], s5p[:, 32:48]
        s5q = [small(16) for _ in range(14)]
        chp = small(MT * 10)
        pcol = {n: chp[:, i * MT:(i + 1) * MT] for i, n in enumerate(["d", "glu_b", "conv_b", "ba", "bi", "lam"])}
        convw = [chp[:, (6 + k) * MT:(7 + k) * MT] for k in range(4)]
        cl, cneg = small(MT), small(MT)
        l1, l2 = small(MT), small(MT)
        bre = rega[:, 0:256].rearrange("p (s h) -> p s h", s=NS5)
        bim = rega[:, 256:512].rearrange("p (s h) -> p s h", s=NS5)
        bdre = rega[:, 512:1024].rearrange("p (s h) -> p s h", s=NS5)
        bdim = rega[:, 1024:1536].rearrange("p (s h) -> p s h", s=NS5)
        btmp = rega[:, 1536:1792].rearrange("p (s h) -> p s h", s=NS5)
        btmp2 = rega[:, 1792:2048].rearrange("p (s h) -> p s h", s=NS5)

        s_ev_x = [sem(f"s_wevin{i}") for i in range(3)]
        s_pj = sem("s_pj")
        s_pje = sem("s_pje")
        s_conv = sem("s_conv")
        s_gt = sem("s_gt")
        s_gts = sem("s_gts")
        s_lb = sem("s_lb")
        s_ab = sem("s_ab")
        s_q1 = sem("s_q1")
        s_q2 = sem("s_q2")
        s_xpad = sem("s_xpad")
        s_prm = sem("s_prm")
        s_pra = sem("s_pra")
        s_brd = sem("s_brd")
        s_btr = sem("s_btr")
        s_bte = sem("s_bte")
        s_bu = sem("s_bu")
        s_ph = sem("s_ph")
        s_sn = sem("s_sn")
        s_tab = sem("s_tab")
        s_pre = sem("s_pre")
        s_z = sem("s_z")
        s_st = sem("s_st")
        s_cy = sem("s_cy")
        s_yd = sem("s_yd")
        s_yg = sem("s_yg")
        s_gl = sem("s_gl")
        s_gs = sem("s_gs")
        s_ya = sem("s_ya")
        s_yb = sem("s_yb")
        s_op = sem("s_op")
        s_xr = sem("s_xr")

        ORDER = [4, 5, 6, 7, 0, 1, 2, 3, 8, 9, 10, 11]
        wcol = [wbuf[:, i * 4096:(i + 1) * 4096].rearrange("p (k n) -> p k n", k=KC) for i in range(2)]

        def even_tensor():
            def project(n):
                m = ORDER[n]
                if n % 4 == 0:
                    TE.wait_ge(s_ev_x[n // 4], 16)
                if n >= 2:
                    TE.wait_ge(s_pje, n - 1)
                w = wcol[(n // 4) % 2]
                for k in range(KC):
                    last = TE.matmul(ps[:, n % 2, :], w[:, k, (m % 4) * P:(m % 4 + 1) * P], hT[:, k, :],
                                     start=k == 0, stop=k == KC - 1)
                last.then_inc(s_pj, 1)
            for n in range(8):
                project(n)
            TE.wait_ge(s_brd, 1)
            for q in range(MT):
                for j, b in enumerate((bdre, bdim)):
                    last = TE.transpose(ps[:, 4 + j, q * P:(q + 1) * P],
                                        b[:, 4 * q:4 * q + 4, :].rearrange("p s h -> p (s h)"), ident)
            last.then_inc(s_btr, 1)
            for m in range(MT):
                TE.wait_ge(s_conv, m + 1)
                for j in range(2):
                    if m:
                        TE.wait_ge(s_gts, 2 * (m - 1) + j + 1)
                    for b in range(2):
                        r = slice(64 * b, 64 * b + 64)
                        last = TE.matmul(ps[r, 2 + j, :], lruw[r, j, m, :], xfT[m][r, :], start=True, stop=True)
                    last.then_inc(s_gt, 1)
            for n in range(8, 12):
                project(n)
            TE.wait_ge(s_bte, 1)
            TE.wait_ge(s_pje, 12)

            def bu(s):
                if s >= 2:
                    TE.wait_ge(s_pre, s - 1)
                r = slice(32 * (s % 4), 32 * (s % 4) + 32)
                for j in range(2):
                    last = TE.matmul(ps[:, 4 + 2 * (s % 2) + j, :], bT[r, j, s // 4, :], uT[r, s // 4, :],
                                     start=True, stop=True, tile_position=(32 * (s % 4), 0))
                last.then_inc(s_bu, 1)

            bu(0)
            bu(1)
            for s in range(NS5):
                if s + 2 < NS5:
                    bu(s + 2)
                TE.wait_ge(s_st, s + 1)
                if s % 4 == 0 and s >= 8:
                    TE.wait_ge(s_yd, s // 4 - 1)
                r = slice(32 * (s % 4), 32 * (s % 4) + 32)
                for j, st in enumerate((sre, sim)):
                    last = TE.matmul(ps[r, (s // 4) % 2, :], cmat[:, j, s, :], st[s % 2],
                                     start=j == 0, stop=j == 1)
                last.then_inc(s_cy, 1)
            TE.wait_ge(s_yg, MT)
            for m in range(MT):
                for k in range(MT):
                    last = TE.matmul(ps[:, 4 + m, :], glu[:, k, m * P:(m + 1) * P], yg[:, k, :],
                                     start=k == 0, stop=k == MT - 1)
                last.then_inc(s_gl, 1)
            TE.wait_ge(s_ya, MT)
            TE.wait_ge(s_yb, MT)
            outproj_tensor(0, lambda k, c: uT[:, k, c * P:(c + 1) * P] if k < MT
                           else yl[:, k - MT, c * P:(c + 1) * P])

        def outproj_tensor(layer, lhs):
            base = 8 * layer
            for c in range(TC):
                for nh in range(2):
                    n = 2 * c + nh
                    if c == 0:
                        TE.wait_ge(s_wb[2 * layer + nh], 16)
                    if n >= 4:
                        TE.wait_ge(s_xr, base + n - 3)
                    for k in range(KC):
                        last = TE.matmul(ps[:, n % 4, :], lhs(k, c), wcol[1 - nh][:, k, :],
                                         start=k == 0, stop=k == KC - 1)
                    last.then_inc(s_op, 1)

        def outproj_vector(layer):
            for n in range(8):
                V.wait_ge(s_op, 8 * layer + n + 1)
                xs = x[:, n // 2, (n % 2) * 512:(n % 2 + 1) * 512]
                V.tensor_tensor(xs, ps[:, n % 4, :], xs, ALU.add).then_inc(s_xr, 1)

        def even_scalar():
            S.wait_ge(s_par, 16 * NPAR)
            S.wait_ge(s_prm, 1)
            alink(S.activation(l1, l1, ACT.Exp))
            S.activation(l1, l1, ACT.Ln, bias=1.0).then_inc(s_pra, 1)
            dt_, mag = s5q[0], s5q[1]
            S.activation(dt_, ldt, ACT.Exp).then_inc(s_pra, 1)
            S.wait_ge(s_prm, 2)
            S.activation(mag, s5q[2], ACT.Exp).then_inc(s_pra, 1)
            S.wait_ge(s_prm, 3)
            S.activation(s5q[5], s5q[4], ACT.Sin).then_inc(s_pra, 1)
            S.activation(s5q[6], s5q[4], ACT.Sin, scale=0.5).then_inc(s_pra, 1)
            for n in range(8):
                proj_out(n)
            for m in range(MT):
                for j, (dst, b) in enumerate(((rT, "ba"), (iT, "bi"))):
                    S.wait_ge(s_gt, 2 * m + j + 1)
                    S.activation(dst[:, m, :], ps[:, 2 + j, :], ACT.Sigmoid,
                                 bias=pcol[b][:, m:m + 1]).then_inc(s_gts, 1)
            for n in range(8, 12):
                proj_out(n)
            S.wait_ge(s_lb, 1)
            S.wait_ge(s_gts, 2 * MT)
            for m in range(MT):
                S.wait_ge(s_conv, MT)
                S.activation(xT[:, m, 0:T], rT[:, m, :], ACT.Exp, scale=cl[:, m:m + 1]).then_inc(s_ab, 1)
                S.wait_ge(s_ab, 2 * m + 1)
                S.activation(rT[:, m, :], rT[:, m, :], ACT.Tanh, scale=cneg[:, m:m + 1]).then_inc(s_ab, 1)
            for m in range(MT):
                S.wait_ge(s_q1, m + 1)
                S.activation(rT[:, m, :], rT[:, m, :], ACT.Sqrt, scale=2.0).then_inc(s_q2, 1)
            for s in range(NS5):
                b = s % 2
                S.wait_ge(s_ph, s + 1)
                if s:
                    S.wait_ge(s_tab, s)
                S.activation(sa[b], ph[b], ACT.Sin, scale=math.pi).then_inc(s_sn, 1)
                alink(S.activation(sbb, ph[b], ACT.Abs))
                S.activation(sbb, sbb, ACT.Sin, scale=-math.pi, bias=halfpi).then_inc(s_sn, 1)
                S.wait_ge(s_sn, 3 * s + 2)
                S.activation(ph[b], sa[b], ACT.Square).then_inc(s_sn, 1)
            S.wait_ge(s_st, NS5)
            for m in range(MT):
                S.wait_ge(s_yd, m + 1)
                S.activation(yg[:, m, :], uT[:, m, :], ACT.Gelu_apprx_tanh).then_inc(s_yg, 1)
            for m in range(MT):
                S.wait_ge(s_gl, m + 1)
                S.activation(gT[:, m, :], ps[:, 4 + m, :], ACT.Sigmoid,
                             bias=pcol["glu_b"][:, m:m + 1]).then_inc(s_gs, 1)

        def proj_out(n):
            m = ORDER[n]
            S.wait_ge(s_pj, n + 1)
            if n == 0:
                S.wait_ge(s_xpad, 1)
            if m < 4:
                S.activation(uT[:, m, :], ps[:, n % 2, :], ACT.Copy).then_inc(s_pje, 1)
            elif m < 8:
                S.activation(xT[:, m - 4, 3:3 + T], ps[:, n % 2, :], ACT.Copy).then_inc(s_pje, 1)
            else:
                S.activation(gT[:, m - 8, :], ps[:, n % 2, :], ACT.Gelu_apprx_tanh).then_inc(s_pje, 1)

        def tt(o, p, q, op):
            vlink(V.tensor_tensor(o, p, q, op))

        def ts(o, p, s1, op1, s2=None, op2=None):
            if s2 is None:
                vlink(V.tensor_scalar(o, p, s1, None, op1))
            else:
                vlink(V.tensor_scalar(o, p, s1, s2, op1, op2))

        def stt(o, p, s, q, op1, op2):
            vlink(V.scalar_tensor_tensor(o, p, s, q, op1, op2))

        rho_hi, rho_lo = s5q[12], s5q[13]

        def even_vector():
            V.wait_ge(s_par, 16 * NPAR)
            vlink(V.memset(xT[:, :, 0:3], 0.0))
            V.memset(bdre, 0.0)
            vlink(V.memset(bdim, 0.0))
            V.nop().then_inc(s_xpad, 1)
            lam = pcol["lam"]
            ts(l1, lam, -1.0, ALU.mult)
            tt(l1, l1, lam, ALU.min)
            ts(l2, lam, 0.0, ALU.min)
            V.nop().then_inc(s_prm, 1)
            dt_, mag, ea, th, red, sn, sh = s5q[0:7]
            lr = s5q[7]
            ts(lr, lam_re, -1e-4, ALU.min)
            ts(cmneg, cmneg, -1.0, ALU.mult)
            V.wait_ge(s_pra, 2)
            tt(l1, l2, l1, ALU.subtract)
            ts(cl, l1, 8.0, ALU.mult)
            ts(cneg, l1, -8.0, ALU.mult)
            V.nop().then_inc(s_lb, 1)
            tt(ea, lr, dt_, ALU.mult)
            tt(th, lam_im, dt_, ALU.mult)
            V.nop().then_inc(s_prm, 1)
            k = s5q[8]
            ts(k, th, 1.0 / TWO_PI, ALU.mult, ROUND, ALU.add)
            ts(k, k, -ROUND, ALU.add)
            stt(red, k, -PI_1, th, ALU.mult, ALU.add)
            stt(red, k, -PI_2, red, ALU.mult, ALU.add)
            stt(red, k, -PI_3, red, ALU.mult, ALU.add)
            V.nop().then_inc(s_prm, 1)
            ts(rho_lo, red, 1.0 / TWO_PI, ALU.mult)
            ts(rho_hi, rho_lo, ROUND / 32768.0, ALU.add)
            ts(rho_hi, rho_hi, -ROUND / 32768.0, ALU.add)
            tt(rho_lo, rho_lo, rho_hi, ALU.subtract)
            V.wait_ge(s_pra, 5)
            cs = s5q[8]
            tt(cs, sh, sh, ALU.mult)
            ts(cs, cs, -2.0, ALU.mult, 1.0, ALU.add)
            lbr, lbi, den, fr, fi = s5q[9], s5q[10], s5q[11], s5q[2], s5q[3]
            tt(lbr, mag, cs, ALU.mult)
            tt(lbi, mag, sn, ALU.mult)
            ts(lbr, lbr, -1.0, ALU.add)
            tt(den, lr, lr, ALU.mult)
            tt(fr, lam_im, lam_im, ALU.mult)
            tt(den, den, fr, ALU.add)
            vlink(V.reciprocal(den, den))
            t1, t2 = s5q[5], s5q[6]
            tt(t1, lbr, lr, ALU.mult)
            tt(t2, lbi, lam_im, ALU.mult)
            tt(t1, t1, t2, ALU.add)
            tt(fr, t1, den, ALU.mult)
            tt(t1, lbi, lr, ALU.mult)
            tt(t2, lbr, lam_im, ALU.mult)
            tt(t1, t1, t2, ALU.subtract)
            tt(fi, t1, den, ALU.mult)
            frb = fr[:, :, None].to_broadcast([P, NS5, 16])
            fib = fi[:, :, None].to_broadcast([P, NS5, 16])
            for dst, (b1, b2, op) in ((bdre, (bre, bim, ALU.subtract)), (bdim, (bim, bre, ALU.add))):
                tt(btmp, b1, frb, ALU.mult)
                tt(btmp2, b2, fib, ALU.mult)
                for g in range(2):
                    r = slice(64 * g, 64 * g + 64)
                    tt(dst[r, :, 16 * g:16 * g + 16], btmp[r, :, :], btmp2[r, :, :], op)
            V.nop().then_inc(s_brd, 1)
            for m in range(MT):
                V.wait_ge(s_pje, m + 1)
                ts(xfT[m], xT[:, m, 3:3 + T], convw[3][:, m:m + 1], ALU.mult, pcol["conv_b"][:, m:m + 1], ALU.add)
                for j in range(3):
                    ins = V.scalar_tensor_tensor(xfT[m], xT[:, m, j:j + T], convw[j][:, m:m + 1], xfT[m],
                                                 ALU.mult, ALU.add)
                    if j < 2:
                        vlink(ins)
                ins.then_inc(s_conv, 1)
            V.wait_ge(s_btr, 1)
            V.tensor_copy(bT[:, 0, :, :].rearrange("p q n -> p (q n)"), ps[:, 4, :])
            vlink(V.tensor_copy(bT[:, 1, :, :].rearrange("p q n -> p (q n)"), ps[:, 5, :]))
            V.nop().then_inc(s_bte, 1)
            V.wait_ge(s_conv, MT)
            V.wait_ge(s_xz, 32)
            for m in range(MT):
                V.wait_ge(s_gts, 2 * m + 2)
                tt(xfT[m], iT[:, m, :], xfT[m], ALU.mult)
            for m in range(MT):
                V.wait_ge(s_ab, 2 * m + 2)
                ts(iT[:, m, :], rT[:, m, :], 1.0, ALU.add)
                vlink(V.reciprocal(iT[:, m, :], iT[:, m, :]))
                V.tensor_tensor(rT[:, m, :], rT[:, m, :], iT[:, m, :], ALU.mult).then_inc(s_q1, 1)
            for m in range(MT):
                V.wait_ge(s_q2, m + 1)
                tt(xfT[m], xfT[m], rT[:, m, :], ALU.mult)
                vlink(V.tensor_tensor_scan(iT[:, m, :], xT[:, m, 0:T], xfT[m], 0.0, ALU.mult, ALU.add))
                V.wait_ge(s_pje, 9 + m)
                V.tensor_tensor(yl[:, m, :], iT[:, m, :], gT[:, m, :], ALU.mult).then_inc(s_yb, 1)
            V.wait_ge(s_yb, MT)
            V.wait_ge(s_pj, 12)
            phases(0)
            phases(1)
            for s in range(NS5):
                b = s % 2
                tables(s)
                V.wait_ge(s_bu, s + 1)
                ur, ui = ps[:, 4 + 2 * b, :], ps[:, 5 + 2 * b, :]
                V.tensor_tensor(pa, ur, tabc[b], ALU.mult)
                V.tensor_tensor(pb, ui, tabs[b], ALU.mult)
                V.tensor_tensor(pc, ui, tabc[b], ALU.mult)
                tt(pd, ur, tabs[b], ALU.mult)
                V.nop().then_inc(s_pre, 1)
                V.tensor_tensor(zr, pa, pb, ALU.add)
                tt(zi, pc, pd, ALU.subtract)
                if s >= 2:
                    V.wait_ge(s_st, s - 1)
                dec = mag[:, s:s + 1].to_broadcast([P, T])
                V.tensor_tensor_scan(zre[b], dec, zr, 0.0, ALU.mult, ALU.add)
                vlink(V.tensor_tensor_scan(zim[b], dec, zi, 0.0, ALU.mult, ALU.add))
                V.nop().then_inc(s_z, 1)
                if s + 2 < NS5:
                    phases(s + 2)
                if s % 4 == 3 and s > 3:
                    s5_skip(s // 4 - 1)
            s5_skip(MT - 1)
            for m in range(MT):
                V.wait_ge(s_gs, m + 1)
                V.tensor_tensor(uT[:, m, :], yg[:, m, :], gT[:, m, :], ALU.mult).then_inc(s_ya, 1)
            outproj_vector(0)

        def s5_skip(m):
            V.wait_ge(s_cy, 4 * m + 4)
            V.wait_ge(s_bu, NS5 if m == MT - 1 else 4 * m + 4)
            V.scalar_tensor_tensor(uT[:, m, :], uT[:, m, :], pcol["d"][:, m:m + 1], ps[:, m % 2, :],
                                   ALU.mult, ALU.add).then_inc(s_yd, 1)

        def phases(s):
            b = s % 2
            hi, lo = rho_hi[:, s:s + 1], rho_lo[:, s:s + 1]
            ts(tk, tcount, hi, ALU.mult, ROUND, ALU.add)
            ts(tk, tk, -ROUND, ALU.add)
            stt(tk, tcount, hi, tk, ALU.mult, ALU.subtract)
            V.scalar_tensor_tensor(ph[b], tcount, lo, tk, ALU.mult, ALU.add).then_inc(s_ph, 1)
            V.wait_ge(s_ph, s + 1)

        def tables(s):
            b = s % 2
            V.wait_ge(s_sn, 3 * s + 3)
            if s >= 2:
                V.wait_ge(s_st, s - 1)
            V.tensor_scalar(tabc[b], ph[b], -2.0, 1.0, ALU.mult, ALU.add)
            vlink(V.scalar_tensor_tensor(tabs[b], sa[b], 2.0, sbb, ALU.mult, ALU.mult))
            V.nop().then_inc(s_tab, 1)

        def even_gpsimd():
            for s in range(NS5):
                b = s % 2
                G.wait_ge(s_z, s + 1)
                G.wait_ge(s_tab, s + 1)
                G.tensor_tensor(ga, zre[b], tabc[b], ALU.mult)
                G.tensor_tensor(gb, zim[b], tabs[b], ALU.mult)
                G.tensor_tensor(gc, zre[b], tabs[b], ALU.mult)
                glink(G.tensor_tensor(gd, zim[b], tabc[b], ALU.mult))
                if s >= 2:
                    G.wait_ge(s_cy, s - 1)
                G.tensor_tensor(sre[b], ga, gb, ALU.subtract)
                glink(G.tensor_tensor(sim[b], gc, gd, ALU.add))
                G.nop().then_inc(s_st, 1)

        cmneg = cmat[:, 1, :, :]

        win = wbuf[:, 0:KC * MLA_IN].rearrange("p (k n) -> p k n", k=KC)
        wuq = wbuf[:, 0:3 * H * QK].rearrange("p (k n) -> p k n", k=3)
        wukv = regb[:, :].rearrange("p (k n) -> p k n", k=2)
        vbuf = rega[:, :].rearrange("p (c n) -> p c n", c=TC)
        kTn = r2[:, 0:4096].rearrange("p (h t) -> p h t", h=H)
        kTr = r2[:, 4096:6144].rearrange("p (h t) -> p h t", h=H // 2)
        oT = r3[:, 0:4096].rearrange("p (h t) -> p h t", h=H)
        qTn = r3[:, 4096:5120].rearrange("p (h t) -> p h t", h=H)
        qTr = r3[:, 5120:5632].rearrange("p (h t) -> p h t", h=H // 2)
        cT = r1[:, 0:5 * T].rearrange("p (k t) -> p k t", k=5)
        qi = r1[:, 2560:2560 + H * QK].rearrange("p (h d) -> p h d", h=H)
        ki = r1[:, 4096:4096 + H * NOPE].rearrange("p (h d) -> p h d", h=H)
        rp = r1[:, 5120:6144].rearrange("p (h d) -> p h d", h=2 * H)
        sq = extra[:, 0:1536]
        cbuf = extra[:, 1536:1536 + MLA_IN]
        pr = [r3[:, 5632:6144], extra[:, 2240:2752]]
        pT = [extra[:, 2752:3264], extra[:, 3264:3776]]
        kro = extra[:, 3776:4032].rearrange("p (c d) -> p c d", c=TC)
        half = ROPE // 2
        rt = [sq[:, i * 512:(i + 1) * 512].rearrange("p (h d) -> p h d", h=2 * H) for i in range(3)]
        posi = sb("posi", [P, TC], I32)
        gnq, gnk, gc5 = small(1), small(1), small(5)
        grq, grk = small(ROPE), small(ROPE)
        posf = small(TC)
        ropea, ropek, ropes, ropec = [bT[:, 0, :, :].rearrange("p q n -> p (q n)")[:, i * 128:(i + 1) * 128]
                                      .rearrange("p (c d) -> p c d", c=TC) for i in range(4)]
        css, croot, crs = small(2), small(2), small(2)
        hss, hroot, hrs, krss = small(16), small(16), small(16), small(1)
        mx, nb, rs, ri = small(3), small(3), small(3), small(3)

        s_pos, s_pos2 = sem("s_pos"), sem("s_pos2")
        s_ang, s_rsn, s_rope = sem("s_ang"), sem("s_rsn"), sem("s_rope")
        s_win, s_uq, s_ukv = sem("s_win"), sem("s_uq"), sem("s_ukv")
        s_c = sem("s_c")
        s_cc = sem("s_cc")
        s_css = sem("s_css")
        s_cr = sem("s_cr")
        s_cn = sem("s_cn")
        s_ct = sem("s_ct")
        s_cte = sem("s_cte")
        s_q = sem("s_q")
        s_qe = sem("s_qe")
        s_hsq = sem("s_hsq")
        s_hs = sem("s_hs")
        s_hr = sem("s_hr")
        s_qn = sem("s_qn")
        s_qt = sem("s_qt")
        s_qte = sem("s_qte")
        s_sc = sem("s_sc")
        s_mx = sem("s_mx")
        s_ex = sem("s_ex")
        s_pn = sem("s_pn")
        s_pt = sem("s_pt")
        s_pte = sem("s_pte")
        s_o = sem("s_o")
        s_oe = sem("s_oe")

        def odd_tensor():
            for c in range(TC):
                if c == 0:
                    TE.wait_ge(s_win, 16)
                if c >= 1:
                    TE.wait_ge(s_cc, c)
                for n in range(2):
                    for k in range(KC):
                        last = TE.matmul(ps[:, n, 0:352], hT[:, k, c * P:(c + 1) * P],
                                         win[:, k, n * 352:(n + 1) * 352], start=k == 0, stop=k == KC - 1)
                last.then_inc(s_c, 1)
                if c:
                    odd_ctrans(c - 1)
            odd_ctrans(TC - 1)
            for c in range(TC):
                if c == 0:
                    TE.wait_ge(s_uq, 16)
                    TE.wait_ge(s_ukv, 16)
                    TE.wait_ge(s_cte, TC)
                else:
                    TE.wait_ge(s_oe, 2 * c)
                for n in range(3):
                    for k in range(3):
                        last = TE.matmul(ps[:, n, :], cT[:, k, c * P:(c + 1) * P], wuq[:, k, n * 512:(n + 1) * 512],
                                         start=k == 0, stop=k == 2)
                    last.then_inc(s_q, 1)
                for n in range(4):
                    for k in range(2):
                        last = TE.matmul(ps[:, 3 + n, :], cT[:, 3 + k, c * P:(c + 1) * P],
                                         wukv[:, k, n * 512:(n + 1) * 512], start=k == 0, stop=k == 1)
                    last.then_inc(s_q, 1)
                TE.wait_ge(s_qe, 7 * (c + 1))
                for b in range(6):
                    if b == 0:
                        TE.wait_ge(s_qn, c + 1)
                    for j in range(4):
                        if b < 2:
                            src = qi[:, 4 * b + j, 0:NOPE]
                        elif b < 4:
                            src = ki[:, 4 * (b - 2) + j, :]
                        else:
                            src = rp[:, 8 * (b - 4) + 2 * j:8 * (b - 4) + 2 * j + 2, :].rearrange("p h d -> p (h d)")
                        last = TE.transpose(ps[:, b, j * P:(j + 1) * P], src, ident)
                    last.then_inc(s_qt, 1)
                TE.wait_ge(s_qte, 6 * (c + 1))
                nk = (c + 1) * P
                for i in range(H + 3):
                    if i < H:
                        n = H * c + i
                        if i >= 3:
                            TE.wait_ge(s_ex, n - 2)
                        r = slice(64 * (i % 2), 64 * (i % 2) + 64)
                        o = ps[:, i % 3, 0:nk]
                        TE.matmul(o, qTn[:, i, :], kTn[:, i, 0:nk], start=True, stop=False)
                        TE.matmul(ps[:, i % 3, nk - P:nk], ident, mask, start=False, stop=False)
                        TE.matmul(o, qTr[r, i // 2, :], kTr[r, i // 2, 0:nk], start=False, stop=True)\
                            .then_inc(s_sc, 1)
                    j = i - 2
                    if 0 <= j < H:
                        n = H * c + j
                        TE.wait_ge(s_pn, n + 1)
                        if n >= 2:
                            TE.wait_ge(s_pte, n - 1)
                        for b in range(c + 1):
                            last = TE.transpose(ps[:, 3 + j % 2, b * P:(b + 1) * P],
                                                pr[j % 2][:, b * P:(b + 1) * P], ident)
                        last.then_inc(s_pt, 1)
                    j = i - 3
                    if 0 <= j < H:
                        n = H * c + j
                        TE.wait_ge(s_pte, n + 1)
                        for b in range(c + 1):
                            last = TE.matmul(ps[:, 5 + j // 4, (j % 4) * P:(j % 4 + 1) * P],
                                             vbuf[:, b, j * VD:(j + 1) * VD],
                                             pT[j % 2][:, b * P:(b + 1) * P], start=b == 0, stop=b == c)
                        last.then_inc(s_o, 1)
            TE.wait_ge(s_oe, 2 * TC)
            outproj_tensor(1, lambda k, c: oT[:, k, c * P:(c + 1) * P])

        def odd_ctrans(c):
            TE.wait_ge(s_cn, c + 1)
            if c:
                TE.wait_ge(s_cte, c)
            for k in range(5):
                last = TE.transpose(ps[:, 2 + k // 4, (k % 4) * P:(k % 4 + 1) * P], cbuf[:, k * P:(k + 1) * P], ident)
            last.then_inc(s_ct, 1)

        def odd_scalar():
            S.wait_ge(s_ang, 1)
            S.activation(ropes, ropea, ACT.Sin).then_inc(s_rsn, 1)
            S.activation(ropek, ropea, ACT.Sin, scale=0.5).then_inc(s_rsn, 1)
            for c in range(TC):
                S.wait_ge(s_c, c + 1)
                if c:
                    S.wait_ge(s_ct, c)
                S.activation(cbuf[:, 0:352], ps[:, 0, 0:352], ACT.Copy)
                alink(S.activation(cbuf[:, 352:704], ps[:, 1, 0:352], ACT.Copy))
                S.nop().then_inc(s_cc, 1)
                S.activation(sq[:, 0:QL], cbuf[:, 0:QL], ACT.Square, accum_out=css[:, 0:1], scale=1.0 / math.sqrt(QL))
                alink(S.activation(sq[:, QL:QL + KVL], cbuf[:, QL:QL + KVL], ACT.Square, accum_out=css[:, 1:2],
                                   scale=1.0 / math.sqrt(KVL)))
                S.activation(croot, css, ACT.Sqrt, bias=eps).then_inc(s_cr, 1)
                S.wait_ge(s_ct, c + 1)
                for k in range(5):
                    ins = S.activation(cT[:, k, c * P:(c + 1) * P], ps[:, 2 + k // 4, (k % 4) * P:(k % 4 + 1) * P],
                                       ACT.Copy, scale=gc5[:, k:k + 1])
                alink(ins)
                S.nop().then_inc(s_cte, 1)
            for c in range(TC):
                for n in range(3):
                    S.wait_ge(s_q, 7 * c + n + 1)
                    if c and n == 0:
                        S.wait_ge(s_qt, 6 * c)
                    ins = S.activation(r1[:, 2560 + n * 512:2560 + (n + 1) * 512], ps[:, n, :], ACT.Copy)
                    ins.then_inc(s_qe, 1)
                S.wait_ge(s_qe, 7 * (c + 1))
                if c:
                    S.wait_ge(s_qn, c)
                S.activation(sq, r1[:, 2560:2560 + H * QK], ACT.Square).then_inc(s_hsq, 1)
                S.wait_ge(s_hs, 3 * c + 1)
                S.activation(sq[:, 0:H * NOPE], r1[:, 4096:4096 + H * NOPE], ACT.Square).then_inc(s_hsq, 1)
                S.wait_ge(s_hs, 3 * c + 2)
                S.activation(sq[:, 1024:1024 + ROPE], kro[:, c, :], ACT.Square, accum_out=krss).then_inc(s_hsq, 1)
                S.wait_ge(s_hs, 3 * c + 3)
                S.activation(hroot, hss, ACT.Sqrt, bias=eps, scale=1.0 / QK).then_inc(s_hr, 1)
                for b in range(6):
                    S.wait_ge(s_qt, 6 * c + b + 1)
                    src = ps[:, b, :].rearrange("p (h t) -> p h t", h=4)
                    cc = slice(c * P, (c + 1) * P)
                    if b < 2:
                        S.activation(qTn[:, 4 * b:4 * b + 4, :], src, ACT.Copy, scale=gnq).then_inc(s_qte, 1)
                    elif b < 4:
                        S.activation(kTn[:, 4 * (b - 2):4 * (b - 2) + 4, cc], src, ACT.Copy, scale=gnk)\
                            .then_inc(s_qte, 1)
                    elif b == 4:
                        S.activation(qTr, src, ACT.Copy).then_inc(s_qte, 1)
                    else:
                        S.activation(kTr[:, :, cc], src, ACT.Copy).then_inc(s_qte, 1)
                nk = (c + 1) * P
                for i in range(H + 2):
                    if i < H:
                        n = H * c + i
                        S.wait_ge(s_mx, n + 1)
                        if n >= 2:
                            S.wait_ge(s_pt, n - 1)
                        S.activation(pr[i % 2][:, 0:nk], ps[:, i % 3, 0:nk], ACT.Exp, scale=ATT_SCALE,
                                     bias=nb[:, i % 3:i % 3 + 1], accum_out=rs[:, i % 3:i % 3 + 1]).then_inc(s_ex, 1)
                    j = i - 2
                    if j >= 0:
                        n = H * c + j
                        S.wait_ge(s_pt, n + 1)
                        if n >= 2:
                            S.wait_ge(s_o, n - 1)
                        S.activation(pT[j % 2][:, 0:nk], ps[:, 3 + j % 2, 0:nk], ACT.Copy).then_inc(s_pte, 1)

        def odd_vector():
            V.wait_ge(s_pos, 16)
            V.tensor_copy(posf, posi[:, :]).then_inc(s_ang0, 1)
            V.wait_ge(s_ang0, 1)
            invf = con[:, C_INVF:C_INVF + half][:, None, :].to_broadcast([P, TC, half])
            tt(ropea, posf[:, :, None].to_broadcast([P, TC, half]), invf, ALU.mult)
            ts(ropek, ropea, 1.0 / TWO_PI, ALU.mult, ROUND, ALU.add)
            ts(ropek, ropek, -ROUND, ALU.add)
            for part in (PI_1, PI_2, PI_3):
                stt(ropea, ropek, -part, ropea, ALU.mult, ALU.add)
            V.nop().then_inc(s_ang, 1)
            V.wait_ge(s_rsn, 2)
            tt(ropec, ropek, ropek, ALU.mult)
            ts(ropec, ropec, -2.0, ALU.mult, 1.0, ALU.add)
            for c in range(TC):
                V.wait_ge(s_cr, c + 1)
                vlink(V.reciprocal(crs, croot))
                V.tensor_copy(kro[:, c, :], cbuf[:, QL + KVL:])
                V.tensor_scalar(cbuf[:, 0:QL], cbuf[:, 0:QL], crs[:, 0:1], None, ALU.mult)
                ts(cbuf[:, QL:QL + KVL], cbuf[:, QL:QL + KVL], crs[:, 1:2], ALU.mult)
                V.nop().then_inc(s_cn, 1)
            for c in range(TC):
                for n in range(4):
                    V.wait_ge(s_q, 7 * c + 4 + n)
                    src = ps[:, 3 + n, :].rearrange("p (h d) -> p h d", h=2)
                    V.tensor_copy(ki[:, 2 * n:2 * n + 2, :], src[:, :, 0:NOPE])
                    vlink(V.tensor_copy(vbuf[:, c, 2 * n * VD:(2 * n + 2) * VD].rearrange("p (h d) -> p h d", h=2),
                                        src[:, :, NOPE:NOPE + VD]))
                    V.nop().then_inc(s_qe, 1)
                V.wait_ge(s_hsq, 3 * c + 1)
                vlink(V.reduce_sum(hss[:, 0:8], sq.rearrange("p (h d) -> p h d", h=H), AX.X))
                V.nop().then_inc(s_hs, 1)
                V.wait_ge(s_hsq, 3 * c + 2)
                vlink(V.reduce_sum(hss[:, 8:16], sq[:, 0:H * NOPE].rearrange("p (h d) -> p h d", h=H), AX.X))
                V.nop().then_inc(s_hs, 1)
                V.wait_ge(s_hsq, 3 * c + 3)
                ts(hss[:, 8:16], hss[:, 8:16], krss, ALU.add)
                V.nop().then_inc(s_hs, 1)
                V.wait_ge(s_hr, c + 1)
                vlink(V.reciprocal(hrs, hroot))
                rq = hrs[:, 0:8][:, :, None]
                rk = hrs[:, 8:16][:, :, None]
                V.tensor_tensor(rp[:, 0:8, :], qi[:, :, NOPE:QK], rq.to_broadcast([P, H, ROPE]), ALU.mult)
                V.tensor_tensor(rp[:, 8:16, :], kro[:, c:c + 1, :].to_broadcast([P, H, ROPE]),
                                rk.to_broadcast([P, H, ROPE]), ALU.mult)
                V.tensor_tensor(qi[:, :, 0:NOPE], qi[:, :, 0:NOPE], rq.to_broadcast([P, H, NOPE]), ALU.mult)
                tt(ki, ki, rk.to_broadcast([P, H, NOPE]), ALU.mult)
                V.tensor_tensor(rp[:, 0:8, :], rp[:, 0:8, :], grq[:, None, :].to_broadcast([P, H, ROPE]), ALU.mult)
                tt(rp[:, 8:16, :], rp[:, 8:16, :], grk[:, None, :].to_broadcast([P, H, ROPE]), ALU.mult)
                cb = ropec[:, c:c + 1, :].to_broadcast([P, 2 * H, half])
                snb = ropes[:, c:c + 1, :].to_broadcast([P, 2 * H, half])
                f1, f2 = rp[:, :, 0:half], rp[:, :, half:ROPE]
                V.tensor_tensor(rt[0], f1, snb, ALU.mult)
                tt(rt[1], f2, snb, ALU.mult)
                tt(f1, f1, cb, ALU.mult)
                tt(f2, f2, cb, ALU.mult)
                V.tensor_tensor(f1, f1, rt[1], ALU.subtract)
                tt(f2, f2, rt[0], ALU.add)
                V.nop().then_inc(s_qn, 1)
                nk = (c + 1) * P
                for i in range(H + 4):
                    if i < H:
                        n = H * c + i
                        V.wait_ge(s_sc, n + 1)
                        vlink(V.reduce_max(mx[:, i % 3:i % 3 + 1], ps[:, i % 3, 0:nk], AX.X))
                        if n >= 3:
                            V.wait_ge(s_ex, n - 2)
                        V.tensor_scalar(nb[:, i % 3:i % 3 + 1], mx[:, i % 3:i % 3 + 1], -ATT_SCALE, None, ALU.mult)\
                            .then_inc(s_mx, 1)
                    j = i - 1
                    if 0 <= j < H:
                        n = H * c + j
                        V.wait_ge(s_ex, n + 1)
                        vlink(V.reciprocal(ri[:, j % 3:j % 3 + 1], rs[:, j % 3:j % 3 + 1]))
                        V.tensor_scalar(pr[j % 2][:, 0:nk], pr[j % 2][:, 0:nk], ri[:, j % 3:j % 3 + 1], None,
                                        ALU.mult).then_inc(s_pn, 1)
                    if i == 7 or i == H + 3:
                        b = 0 if i == 7 else 1
                        V.wait_ge(s_o, H * c + 4 * b + 4)
                        V.tensor_copy(oT[:, 4 * b:4 * b + 4, c * P:(c + 1) * P],
                                      ps[:, 5 + b, :].rearrange("p (h t) -> p h t", h=4)).then_inc(s_oe, 1)
            outproj_vector(1)

        s_ang0 = sem("s_ang0")

        rwb = sb("rwb", [P, KC, 72])
        rbias = sb("rbias", [P, 72])
        R = extra[:, 2048:3072]
        R2 = extra[:, 3072:4096]
        lg = R[:, 0:288].rearrange("p (c n) -> p c n", c=TC)
        m1 = R[:, 288:544].rearrange("p (c e) -> p c e", c=TC)
        m2 = R[:, 544:800].rearrange("p (c e) -> p c e", c=TC)
        oh = R[:, 800:832].rearrange("p (c g) -> p c g", c=TC)
        t8 = R[:, 832:864].rearrange("p (c g) -> p c g", c=TC)
        eg = R[:, 864:896].rearrange("p (c g) -> p c g", c=TC)
        o1 = R[:, 896:928].rearrange("p (c g) -> p c g", c=TC)
        o2 = R[:, 928:960].rearrange("p (c g) -> p c g", c=TC)
        cnt, ovb, ovs = R2[:, 0:64], R2[:, 64:128], R2[:, 128:192]
        dst = R2[:, 256:512].rearrange("p (c e) -> p c e", c=TC)
        mm = R2[:, 512:768].rearrange("p (c e) -> p c e", c=TC)
        wk = R2[:, 768:1024].rearrange("p (c e) -> p c e", c=TC)
        gmx, v1, v2, pg, g12, tm, destf = small(4), small(4), small(4), small(4), small(8), small(4), small(8)
        ovf = small(16)
        ovw = extra[0:1, 0:1024].rearrange("p (i e) -> p i e", i=16)

        xin = [regb[:, i * 1024:(i + 1) * 1024] for i in range(2)]
        xtr = [regb[:, 2048 + i * 512:2048 + (i + 1) * 512].rearrange("p (k s) -> p k s", k=KC) for i in range(2)]
        upb = [regb[:, 3072 + i * 512:3072 + (i + 1) * 512] for i in range(2)]
        act_ = [extra[:, i * 128:(i + 1) * 128].rearrange("p (f s) -> p f s", f=FC) for i in range(2)]
        sil = [extra[:, 256 + i * 128:256 + (i + 1) * 128] for i in range(2)]
        yo = [extra[:, 512 + i * 512:512 + (i + 1) * 512] for i in range(2)]
        gath = rega[:, :].rearrange("p (b d) -> p b d", b=4)

        ml = {n: [sem(f"{n}{l}") for l in range(2)] for n in (
            "s_rw", "s_lg", "s_rt", "s_re", "s_rc", "s_dst", "s_disp",
            "s_xtp", "s_xte", "s_up", "s_upe", "s_sm", "s_si", "s_ac", "s_dn", "s_ye",
            "s_ga", "s_gu", "s_ow", "s_ox", "s_ostep", "s_oys")}
        s_xi = [[sem(f"s_xi{l}{j}") for j in range(2)] for l in range(2)]
        s_yst = [[sem(f"s_yst{l}{j}") for j in range(2)] for l in range(2)]
        s_ring = [sem(f"s_ring{b}") for b in range(RING)]

        def route_tensor(l):
            TE.wait_ge(ml["s_rw"][l], 48)
            for c in range(TC):
                for k in range(KC):
                    last = TE.matmul(ps[:, c, 0:72], hT[:, k, c * P:(c + 1) * P], rwb[:, k, :],
                                     start=k == 0, stop=k == KC - 1)
            last.then_inc(ml["s_lg"][l], 1)
            TE.wait_ge(ml["s_rt"][l], 1)
            for c in range(TC):
                for b in range(c + 1):
                    TE.matmul(ps[:, 4, c * NE:(c + 1) * NE], tri if b == c else ones, mm[:, b, :],
                              start=b == 0, stop=b == c)
            for c in range(TC):
                last = TE.matmul(ps[:, 5, 0:NE], ones, mm[:, c, :], start=c == 0, stop=c == TC - 1)
            last.then_inc(ml["s_rc"][l], 1)

        def first_max(oneh, val, best):
            vlink(V.reduce_max(best, val, AX.X))
            tt(t8, val, best[:, :, None].to_broadcast([P, TC, 8]), ALU.is_equal)
            tt(t8, t8, con[:, C_DESC:C_DESC + 8][:, None, :].to_broadcast([P, TC, 8]), ALU.mult)
            vlink(V.reduce_max(tm, t8, AX.X))
            tt(oneh, t8, tm[:, :, None].to_broadcast([P, TC, 8]), ALU.is_equal)

        def route_vector(l):
            V.wait_ge(ml["s_lg"][l], 1)
            tt(lg, ps[:, 0:4, 0:72], rbias[:, None, :].to_broadcast([P, TC, 72]), ALU.add)
            gl = lg[:, :, 0:8]
            first_max(oh, gl, gmx)
            tt(t8, gl, gmx[:, :, None].to_broadcast([P, TC, 8]), ALU.subtract)
            V.nop().then_inc(ml["s_rt"][l + 0] if False else ml["s_gu"][l], 1)
            el = lg[:, :, 8:72].rearrange("p c (g e) -> p c g e", g=NG)
            for c in range(TC):
                w4 = wk[:, c, :].rearrange("p (g e) -> p g e", g=NG)
                tt(w4, el[:, c, :, :], oh[:, c, :][:, :, None].to_broadcast([P, NG, EG]), ALU.mult)
                vlink(V.reduce_sum(eg[:, c, :], w4.rearrange("p g e -> p e g"), AX.X))
            V.wait_ge(ml["s_re"][l], 1)
            vlink(V.reduce_sum(pg, o2, AX.X))
            vlink(V.reciprocal(pg, pg))
            first_max(o1, eg, v1)
            stt(eg, o1, -1e30, eg, ALU.mult, ALU.add)
            first_max(o2, eg, v2)
            tt(tm, v2, v1, ALU.subtract)
            V.nop().then_inc(ml["s_gu"][l], 1)
            for m, o in ((m1, o1), (m2, o2)):
                for c in range(TC):
                    tt(m[:, c, :].rearrange("p (g e) -> p g e", g=NG),
                       oh[:, c, :][:, :, None].to_broadcast([P, NG, EG]),
                       o[:, c:c + 1, :].to_broadcast([P, NG, EG]), ALU.mult)
            tt(mm, m1, m2, ALU.add)
            V.nop().then_inc(ml["s_rt"][l], 1)
            V.wait_ge(ml["s_re"][l], 2)
            ts(v2, v1, 1.0, ALU.add)
            vlink(V.reciprocal(v2, v2))
            tt(g12[:, 0:4], pg, v2, ALU.mult)
            tt(g12[:, 4:8], g12[:, 0:4], v1, ALU.mult)
            V.wait_ge(ml["s_rc"][l], 1)
            vlink(V.tensor_copy(cnt, ps[:, 5, 0:NE]))
            ts(ovb, cnt, float(CAP), ALU.is_gt)
            for j in range(2, T // CAP):
                stt(ovb, cnt, float(CAP * j), ovb, ALU.is_gt, ALU.add)
            vlink(V.tensor_tensor_scan(ovs, ones[:, 0:NE], ovb, 0.0, ALU.mult, ALU.add))
            tt(ovw[:, :, :], ovs[0:1, None, :].to_broadcast([1, 16, NE]),
               con[0:1, C_I:C_I + 16][:, :, None].to_broadcast([1, 16, NE]), ALU.is_le)
            vlink(V.reduce_sum(ovf[0:1, :], ovw[:, :, :], AX.X))
            ts(ovf[0:1, :], ovf[0:1, :], float(NE - 1), ALU.min)
            vlink(V.tensor_copy(ovf[0:1, 15:16], ovs[0:1, NE - 1:NE]))
            vlink(V.tensor_copy(ovi[0:1, :], ovf[0:1, :]))
            tt(ovs, ovs, ovb, ALU.subtract)
            ts(ovs, ovs, float(NE - 1), ALU.add, float(CAP), ALU.mult)
            tt(ovs, ovs, con[:, C_E:C_E + NE], ALU.subtract)
            rk = ps[:, 4, 0:TC * NE].rearrange("p (c e) -> p c e", c=TC)
            ts(wk, rk, float(CAP), ALU.is_ge)
            tt(wk, wk, ovs[:, None, :].to_broadcast([P, TC, NE]), ALU.mult)
            tt(dst, rk, wk, ALU.add)
            tt(dst, dst, con[:, C_E:C_E + NE][:, None, :].to_broadcast([P, TC, NE]), ALU.add)
            for j, m in enumerate((m1, m2)):
                tt(m, m, dst, ALU.mult)
                vlink(V.reduce_sum(destf[:, 4 * j:4 * j + 4], m, AX.X))
            vlink(V.tensor_copy(idx[:, :], destf))
            V.nop().then_inc(ml["s_dst"][l], 1)

        def route_scalar(l):
            S.wait_ge(ml["s_gu"][l], 1)
            S.activation(o2, t8, ACT.Exp).then_inc(ml["s_re"][l], 1)
            S.wait_ge(ml["s_gu"][l], 2)
            S.activation(v1, tm, ACT.Exp).then_inc(ml["s_re"][l], 1)

        def route_gpsimd(l):
            G.wait_ge(ml["s_dst"][l], 1)
            if l == 0:
                G.wait_ge(s_xz, 32)
            for j in range(8):
                G.indirect_dma_start(xdisp[:, :], bass.IndirectOffsetOnAxis(ap=idx[:, j:j + 1], axis=0),
                                     h[:, j % 4, :], None).then_inc(ml["s_disp"][l], 16)

        def ex_xin(l, e, j):
            S.dma_start(xin[j][0:CAP, :], xdisp[bass.ds(e * CAP, CAP), :]).then_inc(s_xi[l][j], 16)

        def te_xtrans(l, e, j, first):
            TE.wait_ge(s_xi[l][j], 8 * (e - j) + 16)
            if not first:
                TE.wait_ge(ml["s_xte"][l], e - 1)
            TE.sem_inc(s_gate4, 1)
            for k in range(KC):
                last = TE.transpose(ps[:, j, k * CAP:(k + 1) * CAP],
                                    xin[j][0:CAP, :].rearrange("p (q k) -> p k q", k=KC)[:, k, :],
                                    ident[0:CAP, 0:CAP])
            last.then_inc(ml["s_xtp"][l], 1)

        def te_up(l, e, j, b, ringw, first):
            TE.wait_ge(ml["s_xte"][l], e + 1)
            TE.wait_ge(s_ring[b], ringw)
            if not first:
                TE.wait_ge(ml["s_upe"][l], e - 1)
            w = ring[b][:, 0:2, :].rearrange("p a (k f) -> p k a f", k=KC)
            for k in range(KC):
                g = k % 2
                last = TE.matmul(ps[64 * g:64 * g + 64, 2 + j, :], xtr[j][:, k, :], w[:, k, :, :],
                                 start=k < 2, stop=k >= KC - 2)
            last.then_inc(ml["s_up"][l], 1)

        def te_sum(l, e, j, first):
            TE.wait_ge(ml["s_upe"][l], e + 1)
            if not first:
                TE.wait_ge(ml["s_ac"][l], e - 1)
            for a2 in range(2):
                for f in range(FC):
                    src = upb[j][:, a2 * DE:(a2 + 1) * DE].rearrange("p (q f) -> p f q", f=FC)[:, f, :]
                    n = a2 * FC + f
                    last = TE.matmul(ps[:, 4 + j, n * CAP:(n + 1) * CAP], src, id2, start=True, stop=True)
            last.then_inc(ml["s_sm"][l], 1)

        def te_down(l, e, j, b, first):
            TE.wait_ge(ml["s_ac"][l], e + 1)
            if not first:
                TE.wait_ge(ml["s_ye"][l], e - 1)
            for f in range(FC):
                for nh in range(2):
                    last = TE.matmul(ps[64 * nh:64 * nh + 64, 6 + j, :], act_[j][:, f, :],
                                     ring[b][:, 2, f * D + nh * 512:f * D + (nh + 1) * 512],
                                     start=f == 0, stop=f == FC - 1)
            last.then_inc(ml["s_dn"][l], 1)

        def moe_tensor(l):
            te_xtrans(l, 0, 0, True)

            def four(i, first, last):
                for j in range(RING):
                    e = 4 * i + j
                    te_up(l, e, j % 2, j, 48 * (16 * l + i + 1), first and j < 2)
                    if not (last and j == 3):
                        te_xtrans(l, e + 1, (j + 1) % 2, first and j == 0)
                    if not (first and j == 0):
                        te_down(l, e - 1, (j + 1) % 2, (j - 1) % RING, first and j <= 2)
                    te_sum(l, e, j % 2, first and j < 2)
            four(0, True, False)
            with TE.Fori(1, 15) as i:
                four(i, False, False)
            four(15, False, True)
            te_down(l, 63, 1, 3, False)

        def moe_scalar(l):
            S.wait_ge(ml["s_disp"][l], 128)
            ex_xin(l, 0, 0)
            ex_xin(l, 1, 1)

            def one(e, j, first, last):
                S.wait_ge(ml["s_up"][l], e + 1)
                if not first:
                    S.wait_ge(ml["s_sm"][l], e - 1)
                S.activation(upb[j], ps[:, 2 + j, :], ACT.Copy).then_inc(ml["s_upe"][l], 1)
                if not last:
                    S.wait_ge(ml["s_xtp"][l], e + 1)
                    ex_xin(l, e + 2, j)
                S.wait_ge(ml["s_sm"][l], e + 1)
                if not first:
                    S.wait_ge(ml["s_ac"][l], e - 1)
                S.activation(sil[j], ps[:, 4 + j, 0:FC * CAP], ACT.Silu).then_inc(ml["s_si"][l], 1)

            def store(e, j):
                S.wait_ge(ml["s_ye"][l], e + 1)
                for nh in range(2):
                    S.dma_start(ydisp[bass.ds(e * CAP, CAP), nh * 512:(nh + 1) * 512],
                                yo[j][64 * nh:64 * nh + 64, :]).then_inc(s_yst[l][j], 16)

            def four(i, first, last):
                for j in range(4):
                    e = 4 * i + j
                    one(e, j % 2, first and j < 2, last and j >= 2)
                    if not (first and j == 0):
                        store(e - 1, (j + 1) % 2)
            four(0, True, False)
            with S.Fori(1, 15) as i:
                four(i, False, False)
            four(15, False, True)
            store(63, 1)

        def moe_vector(l):
            def xt(e, j, first):
                V.wait_ge(ml["s_xtp"][l], e + 1)
                if not first:
                    V.wait_ge(ml["s_up"][l], e - 1)
                V.tensor_copy(xtr[j].rearrange("p k s -> p (k s)"), ps[:, j, :]).then_inc(ml["s_xte"][l], 1)

            def act(e, j, first):
                V.wait_ge(ml["s_si"][l], e + 1)
                if not first:
                    V.wait_ge(ml["s_dn"][l], e - 1)
                V.tensor_tensor(act_[j].rearrange("p f s -> p (f s)"), sil[j], ps[:, 4 + j, FC * CAP:2 * FC * CAP],
                                ALU.mult).then_inc(ml["s_ac"][l], 1)

            def yout(e, j, first):
                V.wait_ge(ml["s_dn"][l], e + 1)
                if not first:
                    V.wait_ge(s_yst[l][j], 16 * (e - j))
                V.tensor_copy(yo[j], ps[:, 6 + j, :]).then_inc(ml["s_ye"][l], 1)

            xt(0, 0, True)

            def four(i, first, last):
                for j in range(4):
                    e = 4 * i + j
                    if not (last and j == 3):
                        xt(e + 1, (j + 1) % 2, first and j == 0)
                    if not (first and j == 0):
                        yout(e - 1, (j + 1) % 2, first and j <= 2)
                    act(e, j % 2, first and j < 2)
            four(0, True, False)
            with V.Fori(1, 15) as i:
                four(i, False, False)
            four(15, False, True)
            yout(63, 1, False)

        def expert_weights(b, w, e, s):
            for n, (name, k) in enumerate((("moe_w1", KC), ("moe_w3", KC), ("moe_w2", FC))):
                src = a[name][w][bass.ds(e, 1), :, :].rearrange("a (p k) f -> p (a k f)", k=k)
                nc.sync.dma_start(ring[b][:, n, :], src).then_inc(s, 16)

        def moe_sync(l, ahead):
            SP = nc.sync
            for e in range(ahead, RING):
                expert_weights(e, l, e, s_ring[e])
            with SP.Fori(1, 16) as i:
                for j in range(RING):
                    SP.wait_ge(ml["s_dn"][l], 4 * i + j - 3)
                    SP.sem_inc(s_gate, 1)
                    expert_weights(j, l, 4 * i + j, s_ring[j])

        s_gate = sem("s_gate")

        OX, OXE, OUP, OUE, OSM, OSI, OAC, ODN, OYE = range(1, 10)
        STEPS = 9

        def extra_blocks(eng, l, body):
            nov = eng.value_load(ovi[0:1, 15:16], min_val=0, max_val=OVMAX)
            with eng.Fori(0, OVMAX) as i:
                with eng.If(i < nov):
                    body(i)

        def extra_tensor(l):
            def body(i):
                TE.wait_ge(ml["s_ox"][l], 16 * (i + 1))
                TE.sem_inc(s_gate4, 1)
                for k in range(KC):
                    last = TE.transpose(ps[:, 0, k * CAP:(k + 1) * CAP],
                                        xin[0][0:CAP, :].rearrange("p (q k) -> p k q", k=KC)[:, k, :],
                                        ident[0:CAP, 0:CAP])
                last.then_inc(ml["s_ostep"][l], 1)
                TE.wait_ge(ml["s_ostep"][l], STEPS * i + OXE)
                TE.wait_ge(ml["s_ow"][l], 48 * (i + 1))
                w = ring[0][:, 0:2, :].rearrange("p a (k f) -> p k a f", k=KC)
                for k in range(KC):
                    g = k % 2
                    last = TE.matmul(ps[64 * g:64 * g + 64, 2, :], xtr[0][:, k, :], w[:, k, :, :],
                                     start=k < 2, stop=k >= KC - 2)
                last.then_inc(ml["s_ostep"][l], 1)
                TE.wait_ge(ml["s_ostep"][l], STEPS * i + OUE)
                for n in range(2 * FC):
                    a2, f = n // FC, n % FC
                    src = upb[0][:, a2 * DE:(a2 + 1) * DE].rearrange("p (q f) -> p f q", f=FC)[:, f, :]
                    last = TE.matmul(ps[:, 4, n * CAP:(n + 1) * CAP], src, id2, start=True, stop=True)
                last.then_inc(ml["s_ostep"][l], 1)
                TE.wait_ge(ml["s_ostep"][l], STEPS * i + OAC)
                for f in range(FC):
                    for nh in range(2):
                        last = TE.matmul(ps[64 * nh:64 * nh + 64, 6, :], act_[0][:, f, :],
                                         ring[0][:, 2, f * D + nh * 512:f * D + (nh + 1) * 512],
                                         start=f == 0, stop=f == FC - 1)
                last.then_inc(ml["s_ostep"][l], 1)
            extra_blocks(TE, l, body)

        def extra_scalar(l):
            def body(i):
                S.dma_start(xin[0][0:CAP, :], xdisp[bass.ds((i + NE) * CAP, CAP), :]).then_inc(ml["s_ox"][l], 16)
                S.wait_ge(ml["s_ostep"][l], STEPS * i + OUP)
                S.activation(upb[0], ps[:, 2, :], ACT.Copy).then_inc(ml["s_ostep"][l], 1)
                S.wait_ge(ml["s_ostep"][l], STEPS * i + OSM)
                S.activation(sil[0], ps[:, 4, 0:FC * CAP], ACT.Silu).then_inc(ml["s_ostep"][l], 1)
                S.wait_ge(ml["s_ostep"][l], STEPS * i + OYE)
                for nh in range(2):
                    S.dma_start(ydisp[bass.ds((i + NE) * CAP, CAP), nh * 512:(nh + 1) * 512],
                                yo[0][64 * nh:64 * nh + 64, :]).then_inc(ml["s_oys"][l], 16)
                S.wait_ge(ml["s_oys"][l], 32 * (i + 1))
                S.sem_inc(s_gate3, 1)
            extra_blocks(S, l, body)

        def extra_vector(l):
            def body(i):
                V.wait_ge(ml["s_ostep"][l], STEPS * i + OX)
                V.tensor_copy(xtr[0].rearrange("p k s -> p (k s)"), ps[:, 0, :]).then_inc(ml["s_ostep"][l], 1)
                V.wait_ge(ml["s_ostep"][l], STEPS * i + OSI)
                V.tensor_tensor(act_[0].rearrange("p f s -> p (f s)"), sil[0], ps[:, 4, FC * CAP:2 * FC * CAP],
                                ALU.mult).then_inc(ml["s_ostep"][l], 1)
                V.wait_ge(ml["s_ostep"][l], STEPS * i + ODN)
                V.tensor_copy(yo[0], ps[:, 6, :]).then_inc(ml["s_ostep"][l], 1)
            extra_blocks(V, l, body)

        def extra_gpsimd(l):
            def body(i):
                G.wait_ge(ml["s_oys"][l], 32 * (i + 1))
                G.sem_inc(s_gate2, 1)
            extra_blocks(G, l, body)

        s_gate2, s_gate3, s_gate4 = sem("s_gate2"), sem("s_gate3"), sem("s_gate4")

        def extra_sync(l):
            SP = nc.sync
            SP.wait_ge(ml["s_dst"][l], 1)
            SP.wait_ge(ml["s_dn"][l], NE)

            nov = SP.value_load(ovi[0:1, 15:16], min_val=0, max_val=OVMAX)
            with SP.Fori(0, OVMAX) as i:
                with SP.If(i < nov):
                    e = SP.value_load(ovi[0:1, bass.ds(i, 1)], min_val=0, max_val=NE - 1)
                    expert_weights(0, l, e, ml["s_ow"][l])
                    SP.wait_ge(ml["s_ostep"][l], STEPS * i + ODN)
                    SP.sem_inc(s_gate, 1)


        def combine_gpsimd(l):
            for n in range(8):
                c, k = n // 2, n % 2
                if n >= 4:
                    G.wait_ge(ml["s_ga"][l], n - 3)
                G.indirect_dma_start(gath[:, n % 4, :], None, ydisp[:, :],
                                     bass.IndirectOffsetOnAxis(ap=idx[:, 4 * k + c:4 * k + c + 1], axis=0))\
                    .then_inc(s_gat[n % 4], 16)

        s_gat = [sem(f"s_gat{i}") for i in range(4)]

        def combine_vector(l):
            for n in range(8):
                c, k = n // 2, n % 2
                V.wait_ge(s_gat[n % 4], 16 * (2 * l + n // 4 + 1))
                chain["v"] += 0
                ins = V.scalar_tensor_tensor(x[:, c, :], gath[:, n % 4, :], g12[:, 4 * k + c:4 * k + c + 1],
                                             x[:, c, :], ALU.mult, ALU.add)
                ins.then_inc(ml["s_ga"][l], 1)
                V.wait_ge(ml["s_ga"][l], n + 1)

        PARAMS = [("p_s5", s5p), ("p_ch", chp), ("p_bre", bre), ("p_bim", bim), ("p_gate_w", lruw),
                  ("p_glu_w", glu)]
        NPAR = len(PARAMS) + 4
        yzero = gath[:, 3:4, :]

        block = ctx.enter_context(nc.Block())

        @block.sync
        def _(sp):
            sp.dma_start(con[:, :], a["p_const"]).then_inc(s_con, 16)
            for c in range(TC):
                sp.dma_start(x[:, c, :], a["x"][c * P:(c + 1) * P, :]).then_inc(s_x, 16)
            wv = a["ev_w_in"].rearrange("(p k) n -> p k n", k=KC)
            for n, j in enumerate((1, 0)):
                sp.dma_start(wcol[n], wv[:, :, j * 512:(j + 1) * 512]).then_inc(s_ev_x[n], 16)
            expert_weights(0, 0, 0, s_ring[0])
            expert_weights(1, 0, 1, s_ring[1])
            sp.wait_ge(s_zero, 1)
            sp.dma_start(xdisp.rearrange("(n p) d -> p n d", p=P),
                         yzero.to_broadcast([P, NBLK * CAP // P, D])).then_inc(s_xz, 16)
            sp.dma_start(ydisp[NE * CAP:, :].rearrange("(n p) d -> p n d", p=P),
                         yzero.to_broadcast([P, (NBLK - NE) * CAP // P, D])).then_inc(s_xz, 16)
            sp.wait_ge(s_pj, 4)
            sp.dma_start(wcol[0], wv[:, :, 1024:1536]).then_inc(s_ev_x[2], 16)
            wo = a["ev_w_out"].rearrange("(k p) n -> p k n", p=P)
            sp.wait_ge(s_pj, 8)
            sp.dma_start(wcol[1], wo[:, :, 0:512]).then_inc(s_wb[0], 16)
            sp.wait_ge(s_pj, 12)
            sp.dma_start(wcol[0], wo[:, :, 512:1024]).then_inc(s_wb[1], 16)
            sp.wait_ge(s_bar, 4)
            expert_weights(2, 0, 2, s_ring[2])
            expert_weights(3, 0, 3, s_ring[3])
            sp.dma_start(win, a["mla_w_in"].rearrange("(p k) n -> p k n", k=KC)).then_inc(s_win, 16)
            moe_sync(0, 4)
            extra_sync(0)
            sp.wait_ge(s_bar, 8)
            expert_weights(0, 1, 0, s_ring[0])
            sp.wait_ge(s_c, TC)
            sp.dma_start(wuq, a["mla_w_uq"].rearrange("(k p) n -> p k n", p=P)).then_inc(s_uq, 16)
            sp.dma_start(wukv, a["mla_w_ukv"].rearrange("(k p) n -> p k n", p=P)).then_inc(s_ukv, 16)
            sp.wait_ge(s_q, 7 * TC)
            wo = a["mla_w_o"].rearrange("(k p) n -> p k n", p=P)
            sp.dma_start(wcol[1], wo[:, :, 0:512]).then_inc(s_wb[2], 16)
            sp.dma_start(wcol[0], wo[:, :, 512:1024]).then_inc(s_wb[3], 16)
            sp.wait_ge(s_bar, 12)
            moe_sync(1, 1)
            extra_sync(1)
            sp.wait_ge(ml["s_ga"][1], 8)
            sp.dma_start(out.rearrange("(c p) d -> p c d", p=P), x[:, :, :]).then_inc(s_out, 16)
            sp.wait_ge(s_out, 16)
            for l in range(2):
                for j in range(2):
                    sp.wait_ge(s_yst[l][j], 16 * NE)

        @block.gpsimd
        def _(g):
            def row_gain(n):
                if n:
                    g.wait_ge(s_h, TC * n)
                g.dma_start(gain[:, :], a["p_norms"][n:n + 1, :].to_broadcast([P, D])).then_inc(s_gain, 16)

            def router(l):
                src = a["moe_w_group"][l].rearrange("(p k) n -> p k n", k=KC)
                g.dma_start(rwb[:, :, 0:8], src).then_inc(ml["s_rw"][l], 16)
                src = a["moe_w_expert"][l].rearrange("(p k) n -> p k n", k=KC)
                g.dma_start(rwb[:, :, 8:72], src).then_inc(ml["s_rw"][l], 16)
                g.dma_start(rbias[:, :], a["p_rbias"][l:l + 1, :].to_broadcast([P, 72])).then_inc(ml["s_rw"][l], 16)

            row_gain(0)
            router(0)
            glink(g.memset(cmat[:, :, :, :], 0.0))
            g.wait_ge(s_tr, TC)
            g.memset(yzero, 0.0).then_inc(s_zero, 1)
            for name, dst_ in PARAMS:
                g.dma_start(dst_, a[name]).then_inc(s_par, 16)
            for j in range(2):
                for q in range(2):
                    r = slice(64 * q, 64 * q + 64)
                    g.dma_start(cmat[r, j, :, 16 * q:16 * q + 16], a["p_c"][j, r, :, :]).then_inc(s_par, 16)
            even_gpsimd()
            g.wait_ge(s_bu, NS5)
            row_gain(1)
            barrier(g, 1)
            for l in range(2):
                if l:
                    pass
                route_gpsimd(l)
                if l == 0:
                    g.wait_ge(s_h, 2 * TC)
                    row_gain(2)
                    g.dma_start(posi[:, :], a["p_pos"]).then_inc(s_pos, 16)
                    for d_, nm in ((gnq, "p_gnq"), (gnk, "p_gnk"), (gc5, "p_gc5")):
                        g.dma_start(d_, a[nm]).then_inc(s_pos2, 16)
                    for d_, nm in ((grq, "p_grq"), (grk, "p_grk")):
                        g.dma_start(d_, a[nm].to_broadcast([P, ROPE])).then_inc(s_pos2, 16)
                g.wait_ge(ml["s_disp"][l], 128)
                for j in range(2):
                    g.wait_ge(s_yst[l][j], 16 * NE)
                extra_gpsimd(l)
                combine_gpsimd(l)
                g.wait_ge(ml["s_ga"][l], 8)
                barrier(g, 2 + 2 * l)
                if l == 0:
                    router(1)
                    g.wait_ge(s_qn, TC)
                    row_gain(3)
                    barrier(g, 3)

        @block.scalar
        def _(act):
            act.wait_ge(s_eps, 1)
            act.wait_ge(s_x, 16 * TC)
            norm_scalar(0)
            even_scalar()
            barrier(act, 1)
            for l in range(2):
                norm_scalar(1 + 2 * l)
                route_scalar(l)
                moe_scalar(l)
                for j in range(2):
                    act.wait_ge(s_yst[l][j], 16 * NE)
                extra_scalar(l)
                barrier(act, 2 + 2 * l)
                if l == 0:
                    norm_scalar(2)
                    act.wait_ge(s_pos2, 80)
                    odd_scalar()
                    barrier(act, 3)

        @block.vector
        def _(v):
            v.memset(eps, EPS)
            vlink(v.memset(halfpi, math.pi / 2))
            v.nop().then_inc(s_eps, 1)
            v.wait_ge(s_x, 16 * TC)
            v.wait_ge(s_con, 16)
            norm_vector(0)
            even_vector()
            barrier(v, 1)
            for l in range(2):
                norm_vector(1 + 2 * l)
                route_vector(l)
                v.wait_ge(ml["s_disp"][l], 128)
                moe_vector(l)
                extra_vector(l)
                combine_vector(l)
                barrier(v, 2 + 2 * l)
                if l == 0:
                    norm_vector(2)
                    v.wait_ge(s_pos2, 80)
                    odd_vector()
                    barrier(v, 3)

        @block.tensor
        def _(t):
            t.wait_ge(s_con, 16)
            norm_tensor(0)
            t.wait_ge(s_par, 16 * NPAR)
            even_tensor()
            barrier(t, 1)
            for l in range(2):
                norm_tensor(1 + 2 * l)
                route_tensor(l)
                moe_tensor(l)
                extra_tensor(l)
                barrier(t, 2 + 2 * l)
                if l == 0:
                    norm_tensor(2)
                    odd_tensor()
                    barrier(t, 3)


def kernel(**inputs):
    import concourse.bacc as _bacc
    from concourse.bass_utils import run_bass_kernel_spmd as _run

    g = {n: np.asarray(v) for n, v in inputs.items()}

    def states(v):
        v = v.reshape((NS5, 2, 64) + v.shape[2:])
        return np.moveaxis(v, 0, 2).reshape((P, NS5) + v.shape[3:])

    def channels(v):
        return v.reshape(MT, P).T

    ldt = np.broadcast_to(g["s5_log_dt"][0][:, None], (32, 64))
    arr = {
        "x": g["x"].reshape(T, D),
        "ev_w_in": g["ev_w_in"][0], "ev_w_out": g["ev_w_out"][0],
        "mla_w_in": g["mla_w_in"][0], "mla_w_uq": g["mla_w_uq"][0],
        "mla_w_ukv": g["mla_w_ukv"][0], "mla_w_o": g["mla_w_o"][0],
        "moe_w_group": g["moe_w_group"], "moe_w_expert": g["moe_w_expert"],
        "moe_w1": g["moe_w1"], "moe_w3": g["moe_w3"], "moe_w2": g["moe_w2"],
        "p_const": shape_constants(),
        "p_norms": np.stack([g["ev_norm"][0], g["ffn_norm"][0], g["od_norm"][0], g["ffn_norm"][1]]),
        "p_rbias": np.concatenate([g["moe_b_group"], g["moe_b_expert"]], axis=1),
        "p_s5": np.concatenate([states(g["s5_lambda_re"][0]), states(g["s5_lambda_im"][0]), states(ldt)], axis=1),
        "p_ch": np.concatenate([channels(g[n][0].reshape(-1)) for n in
                                ("s5_d", "s5_glu_b", "lru_conv_b", "lru_ba", "lru_bi", "lru_lambda")]
                               + [channels(g["lru_conv_w"][0][k]) for k in range(4)], axis=1),
        "p_bre": states(g["s5_b_re"][0]), "p_bim": states(g["s5_b_im"][0]),
        "p_c": np.stack([states(g[n][0].transpose(0, 2, 1)) for n in ("s5_c_re", "s5_c_im")]),
        "p_gate_w": np.stack([g[n][0].reshape(MT, P, 64).transpose(1, 0, 2) for n in ("lru_wa", "lru_wi")], axis=1),
        "p_glu_w": g["s5_glu_w"][0].reshape(MT, P, W5).transpose(1, 0, 2),
        "p_pos": g["positions"].reshape(TC, P).T,
        "p_gnq": g["mla_q_norm"][0][:NOPE].reshape(P, 1), "p_gnk": g["mla_k_norm"][0][:NOPE].reshape(P, 1),
        "p_grq": g["mla_q_norm"][0][NOPE:].reshape(1, ROPE), "p_grk": g["mla_k_norm"][0][NOPE:].reshape(1, ROPE),
        "p_gc5": np.concatenate([g["mla_cq_norm"][0], g["mla_ckv_norm"][0]]).reshape(5, P).T,
    }
    nc = _bacc.Bacc("TRN2", target_bir_lowering=False, num_devices=1)
    arrays, aps = {}, {}
    for name, v in arr.items():
        v = np.ascontiguousarray(v)
        arrays[f"in_{name}"] = v
        aps[name] = nc.dram_tensor(f"in_{name}", v.shape, mybir.dt.from_np(v.dtype), kind="ExternalInput").ap()
    out = nc.dram_tensor("out_0", (T, D), F32, kind="ExternalOutput").ap()
    hybrid_decoder(nc, aps, out)
    r = _run(nc, [arrays], core_ids=[0])
    return r.results[0]["out_0"].reshape(1, T, D)
```

```python
import math
import concourse.bass as bass
from concourse import mybir
from contextlib import ExitStack
import numpy as np

F32 = mybir.dt.float32
I32 = mybir.dt.int32
ALU = mybir.AluOpType
ACT = mybir.ActivationFunctionType
AX = mybir.AxisListType

P = 128
D = 1024
T = 512
TC = T // P
KC = D // P
W5 = 512
MT = W5 // P
NS5 = 16
H = 8
QL, KVL, NOPE, ROPE, VD = 384, 256, 128, 64, 128
QK = NOPE + ROPE
MLA_IN = QL + KVL + ROPE
ATT_SCALE = 1.0 / math.sqrt(QK)
NG, EG = 8, 8
NE = NG * EG
DE = 256
FC = DE // P
CAP = 64
QUART = CAP // 4
OVMAX = 2 * T // CAP - 1
NBLK = NE + OVMAX + 1
EPS = 1e-6
ROUND = 12582912.0
TWO_PI = 2.0 * math.pi
PI_1 = 6.28125
PI_2 = float(np.float32(np.round((TWO_PI - PI_1) * 2.0 ** 22) / 2.0 ** 22))
PI_3 = TWO_PI - PI_1 - PI_2
RING = 4

C_ID, C_UP, C_ONE, C_ID2, C_MASK = 0, 128, 256, 384, 448
C_T, C_E, C_I, C_DESC, C_INVF = 576, 1088, 1152, 1168, 1176
C_ID8 = 1208
C_END = 1216


def shape_constants():
    c = np.zeros((P, C_END), np.float32)
    r = np.arange(P)
    c[:, C_ID:C_ID + P] = np.eye(P)
    c[:, C_UP:C_UP + P] = r[:, None] < r[None, :]
    c[:, C_ONE:C_ONE + P] = 1.0
    c[:, C_ID2:C_ID2 + CAP] = np.eye(CAP)[r % CAP]
    c[:, C_MASK:C_MASK + P] = np.where(r[None, :] <= r[:, None], 0.0, -1e30)
    c[:, C_T:C_T + T] = np.arange(T)
    c[:, C_E:C_E + NE] = np.arange(NE) * CAP
    c[:, C_I:C_I + 16] = np.arange(16)
    c[:, C_DESC:C_DESC + 8] = 8 - np.arange(8)
    c[:, C_INVF:C_INVF + ROPE // 2] = np.float32(1.0) / np.power(
        np.float32(10000.0), np.arange(0, ROPE, 2, dtype=np.float32) / np.float32(ROPE), dtype=np.float32)
    c[:, C_ID8:C_ID8 + 8] = r[:, None] + P * np.arange(8)[None, :] + 1
    return c


def hybrid_decoder(nc, a, out):
    ctx = ExitStack()
    with ctx:
        def sb(name, shape, dt=F32):
            return ctx.enter_context(nc.sbuf_tensor(name, shape, dt))

        def sem(name):
            return ctx.enter_context(nc.semaphore(name))

        ring = [sb(f"ring{b}", [P, 3, KC * DE]) for b in range(RING)]
        x = sb("x", [P, TC, D])
        rega = sb("region_a", [P, TC * D])
        regb = sb("region_b", [P, KC * T])
        wbuf = sb("wbuf", [P, 2 * KC * 512])
        gain = sb("gain", [P, D])
        con = sb("con", [P, C_END])
        extra = sb("extra", [P, 4096])
        smalls = sb("smalls", [P, 700])
        blkidx = sb("blkidx", [P, 2, NBLK], I32)
        icol = sb("icol", [P, 4], I32)
        ovi = sb("ovi", [P, 16], I32)
        used = sb("used", [1, NE], I32)
        ps = ctx.enter_context(nc.psum_tensor("ps", [P, 8, 512], F32))

        ident = con[:, C_ID:C_ID + P]
        tri = con[:, C_UP:C_UP + P]
        ones = con[:, C_ONE:C_ONE + P]
        id2 = con[:, C_ID2:C_ID2 + CAP]
        mask = con[:, C_MASK:C_MASK + P]
        tcount = con[:, C_T:C_T + T]

        spot = [0]

        def small(n):
            s = smalls[:, spot[0]:spot[0] + n]
            spot[0] += n
            assert spot[0] <= 700
            return s

        eps = small(1)
        halfpi = small(1)
        ssq, root, rstd = small(4), small(4), small(4)

        h = rega[:, :].rearrange("p (c d) -> p c d", c=TC)
        hT = regb[:, :].rearrange("p (k t) -> p k t", k=KC)
        r2 = ring[2][:, :, :].rearrange("p a b -> p (a b)")
        r3 = ring[3][:, :, :].rearrange("p a b -> p (a b)")
        r1 = ring[1][:, :, :].rearrange("p a b -> p (a b)")

        hrow = [nc.dram_tensor(f"hrow{l}", [T, D], F32, kind="Internal").ap() for l in range(2)]
        ytok = [nc.dram_tensor(f"ytok{l}", [2 * T, D], F32, kind="Internal").ap() for l in range(2)]

        s_con, s_par = sem("s_con"), sem("s_par")
        s_gain = sem("s_gain")
        s_ssq, s_root = sem("s_ssq"), sem("s_root")
        s_h = sem("s_h")
        s_tr = sem("s_tr")
        s_eva, s_evv = sem("s_eva"), sem("s_evv")
        s_eps = sem("s_eps")
        s_bar = sem("s_bar")
        s_v = sem("s_v")
        s_g = sem("s_g")
        s_a = sem("s_a")
        s_lw = sem("s_lw")
        s_wb = [sem("s_wb0"), sem("s_wb1")]
        s_out = sem("s_out")

        chain = {"v": 0, "g": 0, "a": 0}

        def vlink(ins):
            chain["v"] += 1
            ins.then_inc(s_v, 1)
            nc.vector.wait_ge(s_v, chain["v"])

        def glink(ins):
            chain["g"] += 1
            ins.then_inc(s_g, 1)
            nc.gpsimd.wait_ge(s_g, chain["g"])

        def alink(ins):
            chain["a"] += 1
            ins.then_inc(s_a, 1)
            nc.scalar.wait_ge(s_a, chain["a"])

        def barrier(eng, n):
            eng.drain().then_inc(s_bar, 1)
            eng.wait_ge(s_bar, 4 * n)

        V, S, G, TE = nc.vector, nc.scalar, nc.gpsimd, nc.tensor

        junk = extra[:, 2560:3584]
        s_xr = sem("s_xr")
        s_x = [sem(f"s_x{c}") for c in range(TC)]
        xready = [lambda c: (s_x[c], 16), lambda c: (s_xr, 2 * c + 2),
                  lambda c: (ml["s_ga"][0], 2 * c + 2), lambda c: (s_xr, 8 + 2 * c + 2)]

        def norm_sums(n):
            for c in range(TC):
                S.wait_ge(*xready[n](c))
                S.activation(junk, x[:, c, :], ACT.Square, accum_out=ssq[:, c:c + 1]).then_inc(s_ssq, 1)
                S.wait_ge(s_ssq, TC * n + c + 1)
                S.activation(root[:, c:c + 1], ssq[:, c:c + 1], ACT.Sqrt, bias=eps, scale=1.0 / D)\
                    .then_inc(s_root, 1)

        def norm_scalar(n):
            for c in range(TC):
                S.wait_ge(s_tr, TC * n + c + 1)
                S.activation(hT[:, 0:4, c * P:(c + 1) * P],
                             ps[:, 2 * c, :].rearrange("p (k t) -> p k t", k=4), ACT.Copy).then_inc(s_eva, 1)

        def norm_rows(n, c):
            V.wait_ge(s_root, TC * n + c + 1)
            vlink(V.reciprocal(rstd[:, c:c + 1], root[:, c:c + 1]))
            if c == 0:
                V.wait_ge(s_gain, 16 * (n + 1))
            V.scalar_tensor_tensor(h[:, c, :], x[:, c, :], rstd[:, c:c + 1], gain[:, :],
                                   ALU.mult, ALU.mult).then_inc(s_h, 1)

        def norm_vector(n):
            for c in range(TC):
                V.wait_ge(s_tr, TC * n + c + 1)
                V.tensor_copy(hT[:, 4:8, c * P:(c + 1) * P],
                              ps[:, 2 * c + 1, :].rearrange("p (k t) -> p k t", k=4)).then_inc(s_evv, 1)

        def norm_tensor(n):
            for c in range(TC):
                TE.wait_ge(s_h, TC * n + c + 1)
                hs = h[:, c, :].rearrange("p (q k) -> p k q", k=KC)
                for k in range(KC):
                    last = TE.transpose(ps[:, 2 * c + k // 4, (k % 4) * P:(k % 4 + 1) * P], hs[:, k, :], ident)
                last.then_inc(s_tr, 1)
            TE.wait_ge(s_eva, TC * (n + 1))
            TE.wait_ge(s_evv, TC * (n + 1))

        uT = r2[:, 0:2048].rearrange("p (m t) -> p m t", m=MT)
        gT = r2[:, 2048:4096].rearrange("p (m t) -> p m t", m=MT)
        rT = r2[:, 4096:6144].rearrange("p (m t) -> p m t", m=MT)
        iT = r3[:, 0:2048].rearrange("p (m t) -> p m t", m=MT)
        XW = T + 3
        xT = r3[:, 2048:2048 + MT * XW].rearrange("p (m t) -> p m t", m=MT)
        cmat = r3[:, 4108:5644].rearrange("p (a s h) -> p a s h", a=3, s=NS5)
        lruw = rega[:, 0:512].rearrange("p (a m n) -> p a m n", a=2, m=MT)
        bT = gain[:, :].rearrange("p (a q n) -> p a q n", a=2, q=MT)
        xfT = [extra[:, m * T:(m + 1) * T] for m in range(MT)]
        yl = rega[:, 2048:4096].rearrange("p (m t) -> p m t", m=MT)
        yg = rega[:, 0:2048].rearrange("p (m t) -> p m t", m=MT)
        glu = extra[:, 2048:4096].rearrange("p (k n) -> p k n", k=MT)
        def table(s):
            where = (ring[s // 6][:, :, :].rearrange("p a b -> p (a b)"), s % 6) if s < 12 else (wbuf, s - 8)
            at = 2 * T * where[1]
            return where[0][:, at:at + T], where[0][:, at + T:at + 2 * T]

        LR = [r2[:, 4096 + i * T:4096 + (i + 1) * T] for i in range(4)] + [r3[:, i * T:(i + 1) * T] for i in range(8)]
        RA = [rega[:, i * T:(i + 1) * T] for i in range(8)]
        ph, sa, sbb, tk = RA[4:6], RA[6:8], RA[1:3], RA[3]
        pre = [LR[0:4], xfT]
        zre, zim = LR[4:6], LR[6:8]
        prod = [LR[8:12], RA[0:4]]

        s5p = small(16 * 3)
        lam_re, lam_im, ldt = s5p[:, 0:16], s5p[:, 16:32], s5p[:, 32:48]
        s5q = [small(16) for _ in range(14)]
        chp = small(MT * 10)
        pcol = {n: chp[:, i * MT:(i + 1) * MT] for i, n in enumerate(["d", "glu_b", "conv_b", "ba", "bi", "lam"])}
        convw = [chp[:, (6 + k) * MT:(7 + k) * MT] for k in range(4)]
        cl, cneg = small(MT), small(MT)
        l1, l2 = small(MT), small(MT)
        bre = extra[:, 0:256].rearrange("p (s h) -> p s h", s=NS5)
        bim = extra[:, 256:512].rearrange("p (s h) -> p s h", s=NS5)
        bdre = extra[:, 512:1024].rearrange("p (s h) -> p s h", s=NS5)
        bdim = extra[:, 1024:1536].rearrange("p (s h) -> p s h", s=NS5)
        btmp = extra[:, 1536:1792].rearrange("p (s h) -> p s h", s=NS5)
        btmp2 = extra[:, 1792:2048].rearrange("p (s h) -> p s h", s=NS5)

        s_ev_x = [sem(f"s_wevin{i}") for i in range(3)]
        s_pj = sem("s_pj")
        s_pje = sem("s_pje")
        s_conv = sem("s_conv")
        s_gt = sem("s_gt")
        s_gts = sem("s_gts")
        s_lb = sem("s_lb")
        s_ab = sem("s_ab")
        s_q1 = sem("s_q1")
        s_q2 = sem("s_q2")
        s_xpad = sem("s_xpad")
        s_prm = sem("s_prm")
        s_pra = sem("s_pra")
        s_brd = sem("s_brd")
        s_btr = sem("s_btr")
        s_bte = sem("s_bte")
        s_bu = sem("s_bu")
        s_ph = sem("s_ph")
        s_sn = sem("s_sn")
        s_tab = sem("s_tab")
        s_pre = sem("s_pre")
        s_z = sem("s_z")
        s_st = sem("s_st")
        s_cy = sem("s_cy")
        s_yd = sem("s_yd")
        s_yg = sem("s_yg")
        s_gl = sem("s_gl")
        s_gs = sem("s_gs")
        s_ya = sem("s_ya")
        s_lr = sem("s_lr")
        s_zs = sem("s_zs")
        s_yb = sem("s_yb")
        s_op = sem("s_op")

        PB = [0, 1, 6, 7, 0, 1, 6, 7, 0, 1, 2, 3]
        ORDER = [4, 5, 6, 7, 0, 1, 2, 3, 8, 9, 10, 11]
        wout = [w.rearrange("p (k n) -> p k n", k=KC) for w in (wbuf[:, 0:4096], regb[:, :])]
        wcol = [wbuf[:, i * 4096:(i + 1) * 4096].rearrange("p (k n) -> p k n", k=KC) for i in range(2)]

        def even_tensor():
            def project(n):
                m = ORDER[n]
                if n % 4 == 0:
                    TE.wait_ge(s_ev_x[n // 4], 16)
                if n >= 10:
                    TE.wait_ge(s_gts, 2 * MT)
                elif n >= 4:
                    TE.wait_ge(s_pje, n - 3)
                w = wcol[(n // 4) % 2]
                for k in range(KC):
                    last = TE.matmul(ps[:, PB[n], :], w[:, k, (m % 4) * P:(m % 4 + 1) * P], hT[:, k, :],
                                     start=k == 0, stop=k == KC - 1)
                last.then_inc(s_pj, 1)
            for n in range(4):
                project(n)
            TE.wait_ge(s_brd, 1)
            for q in range(MT):
                for j, b in enumerate((bdre, bdim)):
                    last = TE.transpose(ps[:, 4 + j, q * P:(q + 1) * P],
                                        b[:, 4 * q:4 * q + 4, :].rearrange("p s h -> p (s h)"), ident)
            last.then_inc(s_btr, 1)
            for n in range(4, 9):
                project(n)
            TE.wait_ge(s_lw, 32)
            for m in range(MT):
                TE.wait_ge(s_conv, m + 1)
                for j in range(2):
                    if m:
                        TE.wait_ge(s_gts, 2 * (m - 1) + j + 1)
                    for b in range(2):
                        r = slice(64 * b, 64 * b + 64)
                        last = TE.matmul(ps[r, 2 + j, :], lruw[r, j, m, :], xfT[m][r, :], start=True, stop=True)
                    last.then_inc(s_gt, 1)
            for n in range(9, 12):
                project(n)
            TE.wait_ge(s_bte, 1)
            TE.wait_ge(s_pje, 8)

            def bu(s):
                if s >= 2:
                    TE.wait_ge(s_pre, s - 1)
                r = slice(32 * (s % 4), 32 * (s % 4) + 32)
                for j in range(2):
                    last = TE.matmul(ps[:, 4 + 2 * (s % 2) + j, :], bT[r, j, s // 4, :], uT[r, s // 4, :],
                                     start=True, stop=True, tile_position=(32 * (s % 4), 0))
                last.then_inc(s_bu, 1)

            def out_lru(n):
                for k in range(MT):
                    TE.matmul(ps[:, (n + 2) % 4, :], yl[:, k, (n // 2) * P:(n // 2 + 1) * P],
                              wout[n % 2][:, MT + k, :], start=k == 0, stop=False)

            bu(0)
            bu(1)
            bu(2)
            TE.wait_ge(s_pje, 12)
            for s in range(NS5):
                if s + 3 < NS5:
                    bu(s + 3)
                TE.wait_ge(s_st, s + 1)
                if s % 4 == 0 and s >= 8:
                    TE.wait_ge(s_yd, s // 4 - 1)
                r = slice(32 * (s % 4), 32 * (s % 4) + 32)
                for j, (cm, g) in enumerate(zip((0, 2, 1, 1), prod[s % 2])):
                    last = TE.matmul(ps[r, (s // 4) % 2, :], cmat[:, cm, s, :], g, start=j == 0, stop=j == 3)
                last.then_inc(s_cy, 1)
                if s in (7, 11):
                    TE.wait_ge(s_wb[s // 8], 16)
                    TE.wait_ge(s_yb, MT)
                    out_lru(s // 8)
            TE.wait_ge(s_yg, MT)
            for m in range(MT):
                for k in range(MT):
                    last = TE.matmul(ps[:, 4 + m, :], glu[:, k, m * P:(m + 1) * P], yg[:, k, :],
                                     start=k == 0, stop=k == MT - 1)
                last.then_inc(s_gl, 1)
            out_lru(2)
            out_lru(3)
            TE.wait_ge(s_ya, MT)
            for n in range(8):
                if n >= 4:
                    TE.wait_ge(s_xr, n - 3)
                    out_lru(n)
                for k in range(MT):
                    last = TE.matmul(ps[:, (n + 2) % 4, :], uT[:, k, (n // 2) * P:(n // 2 + 1) * P],
                                     wout[n % 2][:, k, :], start=False, stop=k == MT - 1)
                last.then_inc(s_op, 1)

        def outproj_tensor(lhs):
            for n in range(8):
                if n < 2:
                    TE.wait_ge(s_wb[n], 32)
                if n >= 4:
                    TE.wait_ge(s_xr, 8 + n - 3)
                for k in range(KC):
                    last = TE.matmul(ps[:, (n + 2) % 4, :], lhs(k, n // 2), wout[n % 2][:, k, :],
                                     start=k == 0, stop=k == KC - 1)
                last.then_inc(s_op, 1)

        def outproj_vector(layer):
            for n in range(8):
                V.wait_ge(s_op, 8 * layer + n + 1)
                xs = x[:, n // 2, (n % 2) * 512:(n % 2 + 1) * 512]
                V.tensor_tensor(xs, ps[:, (n + 2) % 4, :], xs, ALU.add).then_inc(s_xr, 1)
                if n in (3, 5):
                    norm_rows(1 + 2 * layer, n // 2 - 1)
            for c in (2, 3):
                norm_rows(1 + 2 * layer, c)

        def even_scalar():
            S.wait_ge(s_par, 16 * NPAR)
            S.wait_ge(s_prm, 1)
            alink(S.activation(l1, l1, ACT.Exp))
            S.activation(l1, l1, ACT.Ln, bias=1.0).then_inc(s_pra, 1)
            dt_, mag = s5q[0], s5q[1]
            S.activation(dt_, ldt, ACT.Exp).then_inc(s_pra, 1)
            S.wait_ge(s_prm, 2)
            S.activation(mag, s5q[2], ACT.Exp).then_inc(s_pra, 1)
            S.wait_ge(s_prm, 3)
            S.activation(s5q[5], s5q[4], ACT.Sin).then_inc(s_pra, 1)
            S.activation(s5q[6], s5q[4], ACT.Sin, scale=0.5).then_inc(s_pra, 1)
            for s in range(12):
                table_scalar(s)
                if s % 2:
                    proj_out(s // 2)
            proj_out(6)
            proj_out(7)
            for m in range(MT):
                for j, (dst, b) in enumerate(((rT, "ba"), (iT, "bi"))):
                    S.wait_ge(s_gt, 2 * m + j + 1)
                    S.activation(dst[:, m, :], ps[:, 2 + j, :], ACT.Sigmoid,
                                 bias=pcol[b][:, m:m + 1]).then_inc(s_gts, 1)
            S.wait_ge(s_lb, 1)
            S.wait_ge(s_gts, 2 * MT)
            for m in range(MT):
                S.wait_ge(s_conv, MT)
                S.activation(xT[:, m, 0:T], rT[:, m, :], ACT.Exp, scale=cl[:, m:m + 1]).then_inc(s_ab, 1)
                S.wait_ge(s_ab, 2 * m + 1)
                S.activation(rT[:, m, :], rT[:, m, :], ACT.Tanh, scale=cneg[:, m:m + 1]).then_inc(s_ab, 1)
            for m in range(MT):
                S.wait_ge(s_q1, m + 1)
                S.activation(rT[:, m, :], rT[:, m, :], ACT.Sqrt).then_inc(s_q2, 1)
            for s in range(12, NS5):
                table_scalar(s)
            for n in range(8, 12):
                proj_out(n)
            S.wait_ge(s_cy, NS5)
            for m in range(MT):
                S.wait_ge(s_yd, m + 1)
                S.activation(yg[:, m, :], uT[:, m, :], ACT.Gelu_apprx_tanh).then_inc(s_yg, 1)
            for m in range(MT):
                S.wait_ge(s_gl, m + 1)
                S.activation(gT[:, m, :], ps[:, 4 + m, :], ACT.Sigmoid,
                             bias=pcol["glu_b"][:, m:m + 1]).then_inc(s_gs, 1)

        def table_scalar(s):
            b = s % 2
            S.wait_ge(s_ph, s + 1)
            if s >= 2:
                S.wait_ge(s_tab, s - 1)
            S.activation(sa[b], ph[b], ACT.Sin, scale=math.pi).then_inc(s_sn, 1)
            alink(S.activation(sbb[b], ph[b], ACT.Abs))
            S.activation(sbb[b], sbb[b], ACT.Sin, scale=-math.pi, bias=halfpi).then_inc(s_sn, 1)
            S.wait_ge(s_sn, 3 * s + 2)
            S.activation(ph[b], sa[b], ACT.Square).then_inc(s_sn, 1)

        def proj_out(n):
            m = ORDER[n]
            S.wait_ge(s_pj, n + 1)
            if n == 0:
                S.wait_ge(s_xpad, 1)
            if m < 4:
                S.activation(uT[:, m, :], ps[:, PB[n], :], ACT.Copy).then_inc(s_pje, 1)
            elif m < 8:
                S.activation(xT[:, m - 4, 3:3 + T], ps[:, PB[n], :], ACT.Copy).then_inc(s_pje, 1)
            else:
                S.activation(gT[:, m - 8, :], ps[:, PB[n], :], ACT.Gelu_apprx_tanh).then_inc(s_pje, 1)

        def tt(o, p, q, op):
            vlink(V.tensor_tensor(o, p, q, op))

        def ts(o, p, s1, op1, s2=None, op2=None):
            if s2 is None:
                vlink(V.tensor_scalar(o, p, s1, None, op1))
            else:
                vlink(V.tensor_scalar(o, p, s1, s2, op1, op2))

        def stt(o, p, s, q, op1, op2):
            vlink(V.scalar_tensor_tensor(o, p, s, q, op1, op2))

        rho_hi, rho_lo = s5q[12], s5q[13]

        def even_vector():
            V.wait_ge(s_par, 16 * NPAR)
            vlink(V.memset(xT[:, :, 0:3], 0.0))
            V.memset(bdre, 0.0)
            vlink(V.memset(bdim, 0.0))
            V.nop().then_inc(s_xpad, 1)
            lam = pcol["lam"]
            ts(l1, lam, -1.0, ALU.mult)
            tt(l1, l1, lam, ALU.min)
            ts(l2, lam, 0.0, ALU.min)
            V.nop().then_inc(s_prm, 1)
            dt_, mag, ea, th, red, sn, sh = s5q[0:7]
            lr = s5q[7]
            ts(lr, lam_re, -1e-4, ALU.min)
            ts(cmat[:, 1, :, :], cmat[:, 1, :, :], -1.0, ALU.mult)
            ts(cmat[:, 2, :, :], cmat[:, 0, :, :], -1.0, ALU.mult)
            V.wait_ge(s_pra, 2)
            tt(l1, l2, l1, ALU.subtract)
            ts(cl, l1, 8.0, ALU.mult)
            ts(cneg, l1, -8.0, ALU.mult)
            V.nop().then_inc(s_lb, 1)
            tt(ea, lr, dt_, ALU.mult)
            tt(th, lam_im, dt_, ALU.mult)
            V.nop().then_inc(s_prm, 1)
            k = s5q[8]
            ts(k, th, 1.0 / TWO_PI, ALU.mult, ROUND, ALU.add)
            ts(k, k, -ROUND, ALU.add)
            stt(red, k, -PI_1, th, ALU.mult, ALU.add)
            stt(red, k, -PI_2, red, ALU.mult, ALU.add)
            stt(red, k, -PI_3, red, ALU.mult, ALU.add)
            V.nop().then_inc(s_prm, 1)
            ts(rho_lo, red, 1.0 / TWO_PI, ALU.mult)
            ts(rho_hi, rho_lo, ROUND / 32768.0, ALU.add)
            ts(rho_hi, rho_hi, -ROUND / 32768.0, ALU.add)
            tt(rho_lo, rho_lo, rho_hi, ALU.subtract)
            V.wait_ge(s_pra, 5)
            cs = s5q[8]
            tt(cs, sh, sh, ALU.mult)
            ts(cs, cs, -2.0, ALU.mult, 1.0, ALU.add)
            lbr, lbi, den, fr, fi = s5q[9], s5q[10], s5q[11], s5q[2], s5q[3]
            tt(lbr, mag, cs, ALU.mult)
            tt(lbi, mag, sn, ALU.mult)
            ts(lbr, lbr, -1.0, ALU.add)
            tt(den, lr, lr, ALU.mult)
            tt(fr, lam_im, lam_im, ALU.mult)
            tt(den, den, fr, ALU.add)
            vlink(V.reciprocal(den, den))
            t1, t2 = s5q[5], s5q[6]
            tt(t1, lbr, lr, ALU.mult)
            tt(t2, lbi, lam_im, ALU.mult)
            tt(t1, t1, t2, ALU.add)
            tt(fr, t1, den, ALU.mult)
            tt(t1, lbi, lr, ALU.mult)
            tt(t2, lbr, lam_im, ALU.mult)
            tt(t1, t1, t2, ALU.subtract)
            tt(fi, t1, den, ALU.mult)
            frb = fr[:, :, None].to_broadcast([P, NS5, 16])
            fib = fi[:, :, None].to_broadcast([P, NS5, 16])
            for dst, (b1, b2, op) in ((bdre, (bre, bim, ALU.subtract)), (bdim, (bim, bre, ALU.add))):
                tt(btmp, b1, frb, ALU.mult)
                tt(btmp2, b2, fib, ALU.mult)
                for g in range(2):
                    r = slice(64 * g, 64 * g + 64)
                    tt(dst[r, :, 16 * g:16 * g + 16], btmp[r, :, :], btmp2[r, :, :], op)
            V.nop().then_inc(s_brd, 1)
            phases(0)
            phases(1)
            for s in range(8):
                tables(s)
                phases(s + 2)
            V.wait_ge(s_btr, 1)
            V.tensor_copy(bT[:, 0, :, :].rearrange("p q n -> p (q n)"), ps[:, 4, :])
            vlink(V.tensor_copy(bT[:, 1, :, :].rearrange("p q n -> p (q n)"), ps[:, 5, :]))
            V.nop().then_inc(s_bte, 1)
            for m in range(MT):
                V.wait_ge(s_pje, m + 1)
                ts(xfT[m], xT[:, m, 3:3 + T], convw[3][:, m:m + 1], ALU.mult, pcol["conv_b"][:, m:m + 1], ALU.add)
                for j in range(3):
                    ins = V.scalar_tensor_tensor(xfT[m], xT[:, m, j:j + T], convw[j][:, m:m + 1], xfT[m],
                                                 ALU.mult, ALU.add)
                    if j < 2:
                        vlink(ins)
                ins.then_inc(s_conv, 1)
            for s in range(8, 12):
                tables(s)
                phases(s + 2)
            for m in range(MT):
                V.wait_ge(s_gts, 2 * m + 2)
                tt(xfT[m], iT[:, m, :], xfT[m], ALU.mult)
            for m in range(MT):
                V.wait_ge(s_ab, 2 * m + 2)
                tt(iT[:, m, :], xT[:, m, 0:T], xT[:, m, 0:T], ALU.mult)
                V.scalar_tensor_tensor(rT[:, m, :], iT[:, m, :], 1.0, rT[:, m, :], ALU.add, ALU.mult)\
                    .then_inc(s_q1, 1)
            for m in range(MT):
                V.wait_ge(s_q2, m + 1)
                tt(xfT[m], xfT[m], rT[:, m, :], ALU.mult)
                V.tensor_tensor_scan(iT[:, m, :], xT[:, m, 0:T], xfT[m], 0.0, ALU.mult, ALU.add)\
                    .then_inc(s_lr, 1)
            V.wait_ge(s_pj, 8)
            for s in range(12, NS5):
                tables(s)
                if s + 2 < NS5:
                    phases(s + 2)
            V.wait_ge(s_lr, MT)
            def products(s):
                tabc, tabs = table(s)
                pa, pb, pc, pd = pre[s % 2]
                V.wait_ge(s_bu, s + 1)
                if s >= 2:
                    V.wait_ge(s_z, s - 1)
                ur, ui = ps[:, 4 + 2 * (s % 2), :], ps[:, 5 + 2 * (s % 2), :]
                V.tensor_tensor(pa, ur, tabc, ALU.mult)
                V.tensor_tensor(pb, ui, tabs, ALU.mult)
                V.tensor_tensor(pc, ui, tabc, ALU.mult)
                V.tensor_tensor(pd, ur, tabs, ALU.mult).then_inc(s_pre, 1)

            products(0)
            for s in range(NS5):
                b = s % 2
                pa, pb, pc, pd = pre[b]
                V.wait_ge(s_pre, s + 1)
                V.tensor_tensor(pa, pa, pb, ALU.add)
                V.tensor_tensor(pc, pc, pd, ALU.subtract).then_inc(s_zs, 1)
                if s + 1 < NS5:
                    products(s + 1)
                V.wait_ge(s_zs, s + 1)
                if s == 0:
                    V.wait_ge(s_yb, MT)
                if s >= 2:
                    V.wait_ge(s_st, s - 1)
                dec = mag[:, s:s + 1].to_broadcast([P, T])
                V.tensor_tensor_scan(zre[b], dec, pa, 0.0, ALU.mult, ALU.add)
                V.tensor_tensor_scan(zim[b], dec, pc, 0.0, ALU.mult, ALU.add).then_inc(s_z, 1)
                if s % 4 == 3 and s > 3:
                    s5_skip(s // 4 - 1)
            s5_skip(MT - 1)
            for m in range(MT):
                V.wait_ge(s_gs, m + 1)
                V.tensor_tensor(uT[:, m, :], yg[:, m, :], gT[:, m, :], ALU.mult).then_inc(s_ya, 1)
            outproj_vector(0)

        def s5_skip(m):
            V.wait_ge(s_cy, 4 * m + 4)
            V.wait_ge(s_bu, NS5 if m == MT - 1 else 4 * m + 4)
            V.scalar_tensor_tensor(uT[:, m, :], uT[:, m, :], pcol["d"][:, m:m + 1], ps[:, m % 2, :],
                                   ALU.mult, ALU.add).then_inc(s_yd, 1)

        def phases(s):
            b = s % 2
            hi, lo = rho_hi[:, s:s + 1], rho_lo[:, s:s + 1]
            ts(tk, tcount, hi, ALU.mult, ROUND, ALU.add)
            ts(tk, tk, -ROUND, ALU.add)
            stt(tk, tcount, hi, tk, ALU.mult, ALU.subtract)
            V.scalar_tensor_tensor(ph[b], tcount, lo, tk, ALU.mult, ALU.add).then_inc(s_ph, 1)
            V.wait_ge(s_ph, s + 1)

        def tables(s):
            b = s % 2
            V.wait_ge(s_sn, 3 * s + 3)
            tabc, tabs = table(s)
            V.tensor_scalar(tabc, ph[b], -2.0, 1.0, ALU.mult, ALU.add)
            vlink(V.scalar_tensor_tensor(tabs, sa[b], 2.0, sbb[b], ALU.mult, ALU.mult))
            V.nop().then_inc(s_tab, 1)

        def even_gpsimd():
            for m in range(MT):
                G.wait_ge(s_lr, m + 1)
                G.wait_ge(s_pje, 9 + m)
                if m == 0:
                    G.wait_ge(s_tab, NS5)
                G.tensor_tensor(yl[:, m, :], iT[:, m, :], gT[:, m, :], ALU.mult).then_inc(s_yb, 1)
            for s in range(NS5):
                b = s % 2
                G.wait_ge(s_z, s + 1)
                tabc, tabs = table(s)
                if s >= 2:
                    G.wait_ge(s_cy, s - 1)
                g = prod[b]
                G.tensor_tensor(g[0], zre[b], tabc, ALU.mult)
                G.tensor_tensor(g[1], zim[b], tabs, ALU.mult)
                G.tensor_tensor(g[2], zre[b], tabs, ALU.mult)
                glink(G.tensor_tensor(g[3], zim[b], tabc, ALU.mult))
                G.nop().then_inc(s_st, 1)

        HW = MLA_IN // 2
        win = [wbuf[:, at:at + KC * HW].rearrange("p (k n) -> p k n", k=KC) for at in (0, 8192 - KC * HW)]
        wuq = wbuf[:, 0:3 * H * QK].rearrange("p (k n) -> p k n", k=3)
        wukv = regb[:, :].rearrange("p (k n) -> p k n", k=2)
        vbuf = rega[:, :].rearrange("p (c n) -> p c n", c=TC)
        kTn = r2[:, 0:4096].rearrange("p (h t) -> p h t", h=H)
        kTr = r2[:, 4096:6144].rearrange("p (h t) -> p h t", h=H // 2)
        oT = r3[:, 0:4096].rearrange("p (h t) -> p h t", h=H)
        r0 = ring[0][:, :, :].rearrange("p a b -> p (a b)")
        qTn = r0[:, 0:4096].rearrange("p (h t) -> p h t", h=H)
        qTr = r0[:, 4096:6144].rearrange("p (h t) -> p h t", h=H // 2)
        cT = r1[:, 0:5 * T].rearrange("p (k t) -> p k t", k=5)
        rows = [r1[:, 2560:6144], r3[:, 0:3584]]
        qif = [r[:, 0:H * QK] for r in rows]
        kif = [r[:, 1536:1536 + H * NOPE] for r in rows]
        qi = [r.rearrange("p (h d) -> p h d", h=H) for r in qif]
        ki = [r.rearrange("p (h d) -> p h d", h=H) for r in kif]
        rp = [r[:, 2560:3584].rearrange("p (h d) -> p h d", h=2 * H) for r in rows]
        sq = extra[:, 0:1536]
        cbuf = extra[:, 1536:1536 + MLA_IN]
        pr = [r3[:, 4096:4608], extra[:, 2240:2752], r3[:, 4608:5120]]
        pT = [extra[:, 2752:3264], extra[:, 3264:3776]]
        kro = extra[:, 3776:4032].rearrange("p (c d) -> p c d", c=TC)
        half = ROPE // 2
        rt = [sq[:, i * 512:(i + 1) * 512].rearrange("p (h d) -> p h d", h=2 * H) for i in range(3)]
        posi = sb("posi", [P, TC], I32)
        gnq, gnk, gc5 = small(1), small(1), small(5)
        grq, grk = small(ROPE), small(ROPE)
        posf = small(TC)
        ropea, ropek, ropes, ropec = [bT[:, 0, :, :].rearrange("p q n -> p (q n)")[:, i * 128:(i + 1) * 128]
                                      .rearrange("p (c d) -> p c d", c=TC) for i in range(4)]
        css, croot, crs = small(2), small(2), small(2)
        hss, hroot, hrs, krss = small(16), small(16), small(16), small(1)
        mx, nb, rs, ri = small(3), small(3), small(3), small(3)

        s_pos, s_pos2 = sem("s_pos"), sem("s_pos2")
        s_ang, s_rsn, s_rope = sem("s_ang"), sem("s_rsn"), sem("s_rope")
        s_win, s_uq, s_ukv = sem("s_win"), sem("s_uq"), sem("s_ukv")
        s_ch = sem("s_ch")
        s_c = sem("s_c")
        s_css = sem("s_css")
        s_cr = sem("s_cr")
        s_cn = sem("s_cn")
        s_ct = sem("s_ct")
        s_cte = sem("s_cte")
        s_q = sem("s_q")
        s_qa, s_qv = sem("s_qa"), sem("s_qv")
        s_hsq = sem("s_hsq")
        s_hs = sem("s_hs")
        s_hr = sem("s_hr")
        s_qn = sem("s_qn")
        s_sc = sem("s_sc")
        s_mx = sem("s_mx")
        s_ex = sem("s_ex")
        s_pn = sem("s_pn")
        s_pt = sem("s_pt")
        s_pte = sem("s_pte")
        s_o = sem("s_o")
        s_oe = sem("s_oe")

        UNITS = []
        for c in range(TC + 1):
            if c < TC:
                UNITS += [("q", c, n) for n in range(3)] + [("kv", c, n) for n in range(4)]
            if c:
                UNITS += [("t", c - 1, n) for n in range(6)]

        def unit(kind, c, n):
            return UNITS.index((kind, c, n))

        def copied(u):
            kv = UNITS[u][0] == "kv"
            return (s_qv if kv else s_qa), sum((x[0] == "kv") == kv for x in UNITS[:u + 1])

        def odd_tensor():
            for n in range(2):
                for c in range(TC):
                    if c == 0:
                        TE.wait_ge(s_win, 32)
                    for k in range(KC):
                        last = TE.matmul(ps[:, 4 * n + c, 0:HW], hT[:, k, c * P:(c + 1) * P], win[n][:, k, :],
                                         start=k == 0, stop=k == KC - 1)
                    last.then_inc((s_ch, s_c)[n], 1)
                    if n and c:
                        odd_ctrans(c - 1)
            odd_ctrans(TC - 1)
            for u, (kind, c, n) in enumerate(UNITS):
                if u == 0:
                    TE.wait_ge(s_uq, 16)
                    TE.wait_ge(s_cte, TC)
                if u == 3:
                    TE.wait_ge(s_ukv, 16)
                if u >= 8:
                    TE.wait_ge(*copied(u - 8))
                bank = ps[:, u % 8, :]
                cc = slice(c * P, (c + 1) * P)
                if kind == "q":
                    for k in range(3):
                        last = TE.matmul(bank, cT[:, k, cc], wuq[:, k, n * 512:(n + 1) * 512],
                                         start=k == 0, stop=k == 2)
                elif kind == "kv":
                    for k in range(2):
                        last = TE.matmul(bank, cT[:, 3 + k, cc], wukv[:, k, n * 512:(n + 1) * 512],
                                         start=k == 0, stop=k == 1)
                else:
                    if n == 0:
                        TE.wait_ge(s_qn, c + 1)
                    for j in range(4):
                        if n < 2:
                            src = qi[c % 2][:, 4 * n + j, 0:NOPE]
                        elif n < 4:
                            src = ki[c % 2][:, 4 * (n - 2) + j, :]
                        else:
                            src = rp[c % 2][:, 8 * (n - 4) + 2 * j:8 * (n - 4) + 2 * j + 2, :]\
                                .rearrange("p h d -> p (h d)")
                        last = TE.transpose(bank[:, j * P:(j + 1) * P], src, ident)
                last.then_inc(s_q, 1)
            for u in range(len(UNITS) - 8, len(UNITS)):
                TE.wait_ge(*copied(u))
            NHD = H * TC
            for n in range(NHD + 3):
                if n < NHD:
                    c, i = n // H, n % H
                    nk = (c + 1) * P
                    if n >= 3:
                        TE.wait_ge(s_ex, n - 2)
                    r = slice(64 * (i % 2), 64 * (i % 2) + 64)
                    cc = slice(c * P, (c + 1) * P)
                    o = ps[:, n % 3, 0:nk]
                    TE.matmul(o, qTn[:, i, cc], kTn[:, i, 0:nk], start=True, stop=False)
                    TE.matmul(ps[:, n % 3, nk - P:nk], ident, mask, start=False, stop=False)
                    TE.matmul(o, qTr[r, i // 2, cc], kTr[r, i // 2, 0:nk], start=False, stop=True)\
                        .then_inc(s_sc, 1)
                m = n - 2
                if 0 <= m < NHD:
                    TE.wait_ge(s_pn, m + 1)
                    if m >= 2:
                        TE.wait_ge(s_pte, m - 1)
                    for b in range(m // H + 1):
                        last = TE.transpose(ps[:, 3 + m % 2, b * P:(b + 1) * P],
                                            pr[m % 3][:, b * P:(b + 1) * P], ident)
                    last.then_inc(s_pt, 1)
                m = n - 3
                if 0 <= m < NHD:
                    c, i = m // H, m % H
                    if m % 4 == 0 and m >= 8:
                        TE.wait_ge(s_oe, m // 4 - 1)
                    TE.wait_ge(s_pte, m + 1)
                    for b in range(c + 1):
                        last = TE.matmul(ps[:, 5 + (m // 4) % 2, (m % 4) * P:(m % 4 + 1) * P],
                                         vbuf[:, b, i * VD:(i + 1) * VD],
                                         pT[m % 2][:, b * P:(b + 1) * P], start=b == 0, stop=b == c)
                    last.then_inc(s_o, 1)
            TE.wait_ge(s_oe, 2 * TC)
            outproj_tensor(lambda k, c: oT[:, k, c * P:(c + 1) * P])

        def odd_ctrans(c):
            TE.wait_ge(s_cn, c + 1)
            for k in range(5):
                last = TE.transpose(ps[:, c + 4 * (k // 4), (k % 4) * P:(k % 4 + 1) * P],
                                    cbuf[:, k * P:(k + 1) * P], ident)
            last.then_inc(s_ct, 1)

        def odd_scalar():
            S.wait_ge(s_ang, 1)
            S.activation(ropes, ropea, ACT.Sin).then_inc(s_rsn, 1)
            S.activation(ropek, ropea, ACT.Sin, scale=0.5).then_inc(s_rsn, 1)
            for c in range(TC):
                S.wait_ge(s_c, c + 1)
                if c:
                    S.wait_ge(s_ct, c)
                S.activation(cbuf[:, 0:HW], ps[:, c, 0:HW], ACT.Copy)
                alink(S.activation(cbuf[:, HW:2 * HW], ps[:, 4 + c, 0:HW], ACT.Copy))
                S.activation(sq[:, 0:QL], cbuf[:, 0:QL], ACT.Square, accum_out=css[:, 0:1], scale=1.0 / math.sqrt(QL))
                alink(S.activation(sq[:, QL:QL + KVL], cbuf[:, QL:QL + KVL], ACT.Square, accum_out=css[:, 1:2],
                                   scale=1.0 / math.sqrt(KVL)))
                S.activation(croot, css, ACT.Sqrt, bias=eps).then_inc(s_cr, 1)
                S.wait_ge(s_ct, c + 1)
                for k in range(5):
                    ins = S.activation(cT[:, k, c * P:(c + 1) * P],
                                       ps[:, c + 4 * (k // 4), (k % 4) * P:(k % 4 + 1) * P],
                                       ACT.Copy, scale=gc5[:, k:k + 1])
                alink(ins)
                S.nop().then_inc(s_cte, 1)
            for kind, c, n in UNITS:
                if kind == "kv":
                    continue
                u = unit(kind, c, n)
                bank = ps[:, u % 8, :]
                S.wait_ge(s_q, u + 1)
                if kind == "q":
                    if c >= 2 and n == 0:
                        S.wait_ge(s_q, unit("t", c - 2, 5) + 1)
                    S.activation(qif[c % 2][:, n * 512:(n + 1) * 512], bank, ACT.Copy).then_inc(s_qa, 1)
                    if n == 2:
                        S.wait_ge(*copied(u))
                        if c:
                            S.wait_ge(s_qn, c)
                        S.activation(sq, qif[c % 2], ACT.Square).then_inc(s_hsq, 1)
                        S.wait_ge(s_hs, 3 * c + 1)
                        S.wait_ge(*copied(unit("kv", c, 3)))
                        S.activation(sq[:, 0:H * NOPE], kif[c % 2], ACT.Square).then_inc(s_hsq, 1)
                        S.wait_ge(s_hs, 3 * c + 2)
                        S.activation(sq[:, 1024:1024 + ROPE], kro[:, c, :], ACT.Square, accum_out=krss)\
                            .then_inc(s_hsq, 1)
                        S.wait_ge(s_hs, 3 * c + 3)
                        S.activation(hroot, hss, ACT.Sqrt, bias=eps, scale=1.0 / QK).then_inc(s_hr, 1)
                    continue
                src = bank.rearrange("p (h t) -> p h t", h=4)
                cc = slice(c * P, (c + 1) * P)
                if n < 2:
                    S.activation(qTn[:, 4 * n:4 * n + 4, cc], src, ACT.Copy, scale=gnq).then_inc(s_qa, 1)
                elif n < 4:
                    S.activation(kTn[:, 4 * (n - 2):4 * (n - 2) + 4, cc], src, ACT.Copy, scale=gnk).then_inc(s_qa, 1)
                else:
                    S.activation((qTr, kTr)[n - 4][:, :, cc], src, ACT.Copy).then_inc(s_qa, 1)
            for n in range(H * TC + 2):
                if n < H * TC:
                    nk = (n // H + 1) * P
                    S.wait_ge(s_mx, n + 1)
                    if n >= 3:
                        S.wait_ge(s_pt, n - 2)
                    S.activation(pr[n % 3][:, 0:nk], ps[:, n % 3, 0:nk], ACT.Exp, scale=ATT_SCALE,
                                 bias=nb[:, n % 3:n % 3 + 1], accum_out=rs[:, n % 3:n % 3 + 1]).then_inc(s_ex, 1)
                m = n - 2
                if m >= 0:
                    nk = (m // H + 1) * P
                    S.wait_ge(s_pt, m + 1)
                    if m >= 2:
                        S.wait_ge(s_o, m - 1)
                    S.activation(pT[m % 2][:, 0:nk], ps[:, 3 + m % 2, 0:nk], ACT.Copy).then_inc(s_pte, 1)

        def odd_vector():
            V.wait_ge(s_pos, 16)
            V.tensor_copy(posf, posi[:, :]).then_inc(s_ang0, 1)
            V.wait_ge(s_ang0, 1)
            invf = con[:, C_INVF:C_INVF + half][:, None, :].to_broadcast([P, TC, half])
            tt(ropea, posf[:, :, None].to_broadcast([P, TC, half]), invf, ALU.mult)
            ts(ropek, ropea, 1.0 / TWO_PI, ALU.mult, ROUND, ALU.add)
            ts(ropek, ropek, -ROUND, ALU.add)
            for part in (PI_1, PI_2, PI_3):
                stt(ropea, ropek, -part, ropea, ALU.mult, ALU.add)
            V.nop().then_inc(s_ang, 1)
            V.wait_ge(s_rsn, 2)
            tt(ropec, ropek, ropek, ALU.mult)
            ts(ropec, ropec, -2.0, ALU.mult, 1.0, ALU.add)
            for c in range(TC):
                V.wait_ge(s_cr, c + 1)
                vlink(V.reciprocal(crs, croot))
                V.tensor_copy(kro[:, c, :], cbuf[:, QL + KVL:])
                V.tensor_scalar(cbuf[:, 0:QL], cbuf[:, 0:QL], crs[:, 0:1], None, ALU.mult)
                ts(cbuf[:, QL:QL + KVL], cbuf[:, QL:QL + KVL], crs[:, 1:2], ALU.mult)
                V.nop().then_inc(s_cn, 1)
            for c in range(TC):
                q_, k_, p_ = qi[c % 2], ki[c % 2], rp[c % 2]
                if c >= 2:
                    V.wait_ge(s_q, unit("t", c - 2, 5) + 1)
                V.wait_ge(s_hsq, 3 * c + 1)
                vlink(V.reduce_sum(hss[:, 0:8], sq.rearrange("p (h d) -> p h d", h=H), AX.X))
                V.nop().then_inc(s_hs, 1)
                for n in range(4):
                    u = unit("kv", c, n)
                    V.wait_ge(s_q, u + 1)
                    src = ps[:, u % 8, :].rearrange("p (h d) -> p h d", h=2)
                    V.tensor_copy(k_[:, 2 * n:2 * n + 2, :], src[:, :, 0:NOPE])
                    V.tensor_copy(vbuf[:, c, 2 * n * VD:(2 * n + 2) * VD].rearrange("p (h d) -> p h d", h=2),
                                  src[:, :, NOPE:NOPE + VD]).then_inc(s_qv, 1)
                V.wait_ge(s_hsq, 3 * c + 2)
                vlink(V.reduce_sum(hss[:, 8:16], sq[:, 0:H * NOPE].rearrange("p (h d) -> p h d", h=H), AX.X))
                V.nop().then_inc(s_hs, 1)
                V.wait_ge(s_hsq, 3 * c + 3)
                ts(hss[:, 8:16], hss[:, 8:16], krss, ALU.add)
                V.nop().then_inc(s_hs, 1)
                V.wait_ge(s_hr, c + 1)
                vlink(V.reciprocal(hrs, hroot))
                rq = hrs[:, 0:8][:, :, None]
                rk = hrs[:, 8:16][:, :, None]
                V.tensor_tensor(p_[:, 0:8, :], q_[:, :, NOPE:QK], rq.to_broadcast([P, H, ROPE]), ALU.mult)
                V.tensor_tensor(p_[:, 8:16, :], kro[:, c:c + 1, :].to_broadcast([P, H, ROPE]),
                                rk.to_broadcast([P, H, ROPE]), ALU.mult)
                V.tensor_tensor(q_[:, :, 0:NOPE], q_[:, :, 0:NOPE], rq.to_broadcast([P, H, NOPE]), ALU.mult)
                tt(k_, k_, rk.to_broadcast([P, H, NOPE]), ALU.mult)
                V.tensor_tensor(p_[:, 0:8, :], p_[:, 0:8, :], grq[:, None, :].to_broadcast([P, H, ROPE]), ALU.mult)
                tt(p_[:, 8:16, :], p_[:, 8:16, :], grk[:, None, :].to_broadcast([P, H, ROPE]), ALU.mult)
                cb = ropec[:, c:c + 1, :].to_broadcast([P, 2 * H, half])
                snb = ropes[:, c:c + 1, :].to_broadcast([P, 2 * H, half])
                f1, f2 = p_[:, :, 0:half], p_[:, :, half:ROPE]
                V.tensor_tensor(rt[0], f1, snb, ALU.mult)
                tt(rt[1], f2, snb, ALU.mult)
                V.tensor_tensor(f1, f1, cb, ALU.mult)
                tt(f2, f2, cb, ALU.mult)
                V.tensor_tensor(f1, f1, rt[1], ALU.subtract)
                tt(f2, f2, rt[0], ALU.add)
                V.nop().then_inc(s_qn, 1)
            for n in range(H * TC + 5):
                if n < H * TC:
                    nk = (n // H + 1) * P
                    b = n % 3
                    V.wait_ge(s_sc, n + 1)
                    vlink(V.reduce_max(mx[:, b:b + 1], ps[:, b, 0:nk], AX.X))
                    if n >= 3:
                        V.wait_ge(s_ex, n - 2)
                    V.tensor_scalar(nb[:, b:b + 1], mx[:, b:b + 1], -ATT_SCALE, None, ALU.mult).then_inc(s_mx, 1)
                m = n - 1
                if 0 <= m < H * TC:
                    b = m % 3
                    V.wait_ge(s_ex, m + 1)
                    vlink(V.reciprocal(ri[:, b:b + 1], rs[:, b:b + 1]))
                    nk = (m // H + 1) * P
                    V.tensor_scalar(pr[b][:, 0:nk], pr[b][:, 0:nk], ri[:, b:b + 1], None, ALU.mult).then_inc(s_pn, 1)
                if n >= 8 and n % 4 == 0:
                    g = n // 4 - 2
                    V.wait_ge(s_o, 4 * g + 4)
                    c, b = g // 2, g % 2
                    V.tensor_copy(oT[:, 4 * b:4 * b + 4, c * P:(c + 1) * P],
                                  ps[:, 5 + g % 2, :].rearrange("p (h t) -> p h t", h=4)).then_inc(s_oe, 1)
            outproj_vector(1)

        s_ang0 = sem("s_ang0")

        rwb = sb("rwb", [P, KC, 72])
        rbias = sb("rbias", [P, 72])
        R = extra[:, 2048:3072]
        R2 = extra[:, 3072:4096]
        lg = R[:, 0:288].rearrange("p (c n) -> p c n", c=TC)
        m1 = R[:, 288:544].rearrange("p (c e) -> p c e", c=TC)
        m2 = R[:, 544:800].rearrange("p (c e) -> p c e", c=TC)
        oh = R[:, 800:832].rearrange("p (c g) -> p c g", c=TC)
        t8 = R[:, 832:864].rearrange("p (c g) -> p c g", c=TC)
        eg = R[:, 864:896].rearrange("p (c g) -> p c g", c=TC)
        o1 = R[:, 896:928].rearrange("p (c g) -> p c g", c=TC)
        o2 = R[:, 928:960].rearrange("p (c g) -> p c g", c=TC)
        ovb, ovs = R2[:, 64:128], R2[:, 128:192]
        m12 = R[:, 288:800].rearrange("p (j e) -> p j e", j=8)
        dst = R2[:, 256:512].rearrange("p (c e) -> p c e", c=TC)
        mm = R2[:, 512:768].rearrange("p (c e) -> p c e", c=TC)
        wk = R2[:, 768:1024].rearrange("p (c e) -> p c e", c=TC)
        gmx, v1, v2, pg, g12, tm = small(4), small(4), small(4), small(4), small(8), small(4)
        destf, blkf, base8 = small(8), small(8), small(8)
        ovf = small(16)
        ovw = rega[0:1, 0:1024].rearrange("p (i e) -> p i e", i=16)

        xin = [regb[:, i * 1024:(i + 1) * 1024] for i in range(2)]
        xtr = [regb[:, 2048 + i * 512:2048 + (i + 1) * 512].rearrange("p (k s) -> p k s", k=KC) for i in range(2)]
        upb = [regb[:, 3072 + i * 512:3072 + (i + 1) * 512] for i in range(2)]
        act_ = [extra[:, i * 128:(i + 1) * 128].rearrange("p (f s) -> p f s", f=FC) for i in range(2)]
        sil = [extra[:, 256 + i * 128:256 + (i + 1) * 128] for i in range(2)]
        yo = [extra[0:CAP, 512 + i * 1024:512 + (i + 1) * 1024] for i in range(2)]
        hot_s = extra[:, 0:8 * CAP].rearrange("p (j s) -> p j s", j=8)
        hot_b = extra[:, 512:512 + 8 * NBLK].rearrange("p (j b) -> p j b", j=8)
        hot8 = extra[:, 0:8 * NE].rearrange("p (j e) -> p j e", j=8)
        gath = rega[:, :].rearrange("p (b d) -> p b d", b=4)

        s_rw = sem("s_rw")
        s_lg = sem("s_lg")
        s_gu = sem("s_gu")
        s_re = sem("s_re")
        s_rt = sem("s_rt")
        s_rc = sem("s_rc")
        s_hot, s_hp = sem("s_hot"), sem("s_hp")
        s_dst = sem("s_dst")
        s_ov = sem("s_ov")
        s_hst = sem("s_hst")
        ml = {n: [sem(f"{n}{l}") for l in range(2)] for n in (
            "s_xtp", "s_xte", "s_up", "s_upe", "s_sm", "s_si", "s_ac", "s_dn", "s_ye", "s_ye2",
            "s_ga", "s_ow", "s_ox", "s_ostep", "s_oys")}
        s_xi = [[sem(f"s_xi{l}{j}") for j in range(2)] for l in range(2)]
        s_yst = [[sem(f"s_yst{l}{j}") for j in range(2)] for l in range(2)]
        s_ring = [sem(f"s_ring{b}") for b in range(RING)]

        def route_tensor(l):
            TE.wait_ge(s_rw, 48 * l + 48)
            for c in range(TC):
                for k in range(KC):
                    last = TE.matmul(ps[:, c, 0:72], hT[:, k, c * P:(c + 1) * P], rwb[:, k, :],
                                     start=k == 0, stop=k == KC - 1)
            last.then_inc(s_lg, 1)
            TE.wait_ge(s_rt, l + 1)
            rk = ps[:, 4, 0:(TC + 1) * NE]
            TE.matmul(rk[:, 0:NE], tri, mm[:, 0, :], start=True, stop=True)
            for b in range(TC):
                last = TE.matmul(rk[:, (b + 1) * NE:], ones, mm[:, b:b + 1, :].to_broadcast([P, TC - b, NE]),
                                 start=b == 0, stop=b == TC - 1)
                if b == TC - 2:
                    TE.matmul(rk[:, NE:TC * NE], tri, mm[:, 1:TC, :], start=False, stop=False)
            last.then_inc(s_rc, 1)

        def table_tensor(l):
            TE.wait_ge(s_hot, l + 1)
            for j in range(8):
                last = TE.matmul(ps[0:CAP, 6, 0:NBLK], hot_s[:, j, :], hot_b[:, j, :], start=j == 0, stop=j == 7)
            last.then_inc(s_hp, 1)

        def first_max(oneh, val, best):
            vlink(V.reduce_max(best, val, AX.X))
            tt(t8, val, best[:, :, None].to_broadcast([P, TC, 8]), ALU.is_equal)
            tt(t8, t8, con[:, C_DESC:C_DESC + 8][:, None, :].to_broadcast([P, TC, 8]), ALU.mult)
            vlink(V.reduce_max(tm, t8, AX.X))
            tt(oneh, t8, tm[:, :, None].to_broadcast([P, TC, 8]), ALU.is_equal)

        def route_vector(l):
            V.wait_ge(s_lg, l + 1)
            tt(lg, ps[:, 0:4, 0:72], rbias[:, None, :].to_broadcast([P, TC, 72]), ALU.add)
            gl = lg[:, :, 0:8]
            first_max(oh, gl, gmx)
            tt(t8, gl, gmx[:, :, None].to_broadcast([P, TC, 8]), ALU.subtract)
            V.nop().then_inc(s_gu, 1)
            el = lg[:, :, 8:72].rearrange("p c (g e) -> p c g e", g=NG)
            w4 = wk[:, :, :].rearrange("p c (g e) -> p c g e", g=NG)
            tt(w4, el, oh[:, :, :, None].to_broadcast([P, TC, NG, EG]), ALU.mult)
            vlink(V.reduce_sum(eg, w4.rearrange("p c g e -> p c e g"), AX.X))
            V.wait_ge(s_re, 2 * l + 1)
            vlink(V.reduce_sum(pg, o2, AX.X))
            vlink(V.reciprocal(pg, pg))
            first_max(o1, eg, v1)
            stt(eg, o1, -1e30, eg, ALU.mult, ALU.add)
            first_max(o2, eg, v2)
            tt(tm, v2, v1, ALU.subtract)
            V.nop().then_inc(s_gu, 1)
            for m, o in ((m1, o1), (m2, o2)):
                tt(m.rearrange("p c (g e) -> p c g e", g=NG), oh[:, :, :, None].to_broadcast([P, TC, NG, EG]),
                   o[:, :, None, :].to_broadcast([P, TC, NG, EG]), ALU.mult)
            tt(mm, m1, m2, ALU.add)
            V.nop().then_inc(s_rt, 1)
            V.wait_ge(s_re, 2 * l + 2)
            ts(v2, v1, 1.0, ALU.add)
            vlink(V.reciprocal(v2, v2))
            tt(g12[:, 0:4], pg, v2, ALU.mult)
            tt(g12[:, 4:8], g12[:, 0:4], v1, ALU.mult)
            tt(hot8, m12, con[:, C_E:C_E + NE][:, None, :].to_broadcast([P, 8, NE]), ALU.mult)
            vlink(V.reduce_sum(base8, hot8, AX.X))
            V.wait_ge(s_rc, l + 1)
            rk = ps[:, 4, 0:TC * NE].rearrange("p (c e) -> p c e", c=TC)
            cnt = ps[:, 4, TC * NE:(TC + 1) * NE]
            ts(ovb, cnt, 1.0 / CAP, ALU.mult, -(CAP + 1) / (2.0 * CAP), ALU.add)
            ts(ovb, ovb, ROUND, ALU.add)
            ts(ovb, ovb, -ROUND, ALU.add, 0.0, ALU.max)
            vlink(V.tensor_tensor_scan(ovs, ones[:, 0:NE], ovb, 0.0, ALU.mult, ALU.add))
            tt(ovb, ovs, ovb, ALU.subtract)
            ts(ovb, ovb, float(NE - 1), ALU.add, float(CAP), ALU.mult)
            tt(ovb, ovb, con[:, C_E:C_E + NE], ALU.subtract)
            ts(wk, rk, float(CAP), ALU.is_ge)
            tt(wk, wk, ovb[:, None, :].to_broadcast([P, TC, NE]), ALU.mult)
            tt(dst, rk, wk, ALU.add)
            m4 = m12.rearrange("p (j c) e -> p j c e", j=2)
            tt(m4, m4, dst[:, None, :, :].to_broadcast([P, 2, TC, NE]), ALU.mult)
            vlink(V.reduce_sum(destf, m12, AX.X))
            tt(destf, destf, base8, ALU.add)
            ts(blkf, destf, 1.0 / CAP, ALU.mult, -(CAP - 1) / (2.0 * CAP), ALU.add)
            ts(blkf, blkf, ROUND, ALU.add)
            ts(blkf, blkf, -ROUND, ALU.add)
            stt(destf, blkf, -float(CAP), destf, ALU.mult, ALU.add)
            for j in range(8):
                V.tensor_scalar(hot_b[:, j, :], tcount[:, 0:NBLK], blkf[:, j:j + 1],
                                con[:, C_ID8 + j:C_ID8 + j + 1], ALU.is_equal, ALU.mult)
            tt(hot_s, tcount[:, None, 0:CAP].to_broadcast([P, 8, CAP]),
               destf[:, :, None].to_broadcast([P, 8, CAP]), ALU.is_equal)
            V.nop().then_inc(s_hot, 1)
            quarters_ = R2[0:1, 0:NE]
            ts(quarters_, cnt[0:1, :], float(QUART), ALU.is_gt)
            for j in range(2, CAP // QUART):
                stt(quarters_, cnt[0:1, :], float(QUART * j), quarters_, ALU.is_gt, ALU.add)
            V.tensor_copy(used[:, :], quarters_)
            V.wait_ge(s_hp, l + 1)
            tb, tg = R[0:CAP, 0:NBLK], R[0:CAP, 128:128 + NBLK]
            ts(tg, ps[0:CAP, 6, 0:NBLK], 0.0, ALU.is_equal, 8.0 * T, ALU.mult)
            stt(tb, ps[0:CAP, 6, 0:NBLK], -1.0, tg, ALU.add, ALU.add)
            ts(tg, tb, float(T), ALU.is_ge, -float(T), ALU.mult)
            tt(tg, tg, tb, ALU.add)
            V.tensor_copy(blkidx[0:CAP, 0, :], tg)
            vlink(V.tensor_copy(blkidx[0:CAP, 1, :], tb))
            V.nop().then_inc(s_dst, 1)
            V.wait_ge(s_hst, 64 * l + 16 * TC)
            tt(ovw[:, :, :], ovs[0:1, None, :].to_broadcast([1, 16, NE]),
               con[0:1, C_I:C_I + 16][:, :, None].to_broadcast([1, 16, NE]), ALU.is_le)
            vlink(V.reduce_sum(ovf[0:1, :], ovw[:, :, :], AX.X))
            ts(ovf[0:1, :], ovf[0:1, :], float(NE - 1), ALU.min)
            vlink(V.tensor_copy(ovf[0:1, 15:16], ovs[0:1, NE - 1:NE]))
            V.tensor_copy(ovi[0:1, :], ovf[0:1, :]).then_inc(s_ov, 1)

        def route_scalar(l):
            S.wait_ge(s_gu, 2 * l + 1)
            S.activation(o2, t8, ACT.Exp).then_inc(s_re, 1)
            S.wait_ge(s_gu, 2 * l + 2)
            S.activation(v1, tm, ACT.Exp).then_inc(s_re, 1)

        def ex_gather(l, e, j, first=False):
            if not first:
                G.wait_ge(ml["s_xtp"][l], e - 1)
                G.sem_inc(s_gate2, 1)
            glink_at(G.tensor_copy(icol[0:CAP, j:j + 1], blkidx[0:CAP, 0, bass.ds(e, 1)]), s_ic[l][0], e + 1)
            def rows(r):
                G.indirect_dma_start(xin[j][r, :], None, hrow[l],
                                     bass.IndirectOffsetOnAxis(ap=icol[r, j:j + 1], axis=0),
                                     bounds_check=T - 1, oob_is_err=False).then_inc(s_xi[l][j], 16)
            quarters(e, rows)

        def ex_scatter(l, e, j):
            G.wait_ge(ml["s_ye"][l], e + 1)
            G.wait_ge(ml["s_ye2"][l], e + 1)
            G.sem_inc(s_gate2, 1)
            glink_at(G.tensor_copy(icol[0:CAP, 2 + j:3 + j], blkidx[0:CAP, 1, bass.ds(e, 1)]), s_ic[l][1], e + 1)
            def rows(r):
                G.indirect_dma_start(ytok[l], bass.IndirectOffsetOnAxis(ap=icol[r, 2 + j:3 + j], axis=0),
                                     yo[j][r, :], None, bounds_check=2 * T - 1, oob_is_err=False)\
                    .then_inc(s_yst[l][j], 16)
            quarters(e, rows)

        def quarters(e, rows):
            n = G.value_load(used[0:1, bass.ds(e, 1)], min_val=0, max_val=CAP // QUART - 1)
            for q in range(CAP // QUART):
                with G.If(n == q):
                    rows(slice(0, QUART * (q + 1)))

        def glink_at(ins, s, n):
            ins.then_inc(s, 1)
            G.wait_ge(s, n)
            G.sem_inc(s_gate2, 1)

        def te_xtrans(l, e, j, first):
            TE.wait_ge(s_xi[l][j], 8 * (e - j) + 16)
            if not first:
                TE.wait_ge(ml["s_xte"][l], e - 1)
            TE.sem_inc(s_gate4, 1)
            for k in range(KC):
                last = TE.transpose(ps[:, j, k * CAP:(k + 1) * CAP],
                                    xin[j][0:CAP, :].rearrange("p (q k) -> p k q", k=KC)[:, k, :],
                                    ident[0:CAP, 0:CAP])
            last.then_inc(ml["s_xtp"][l], 1)

        def te_up(l, e, j, b, ringw, first):
            TE.wait_ge(ml["s_xte"][l], e + 1)
            TE.wait_ge(s_ring[b], ringw)
            if not first:
                TE.wait_ge(ml["s_upe"][l], e - 1)
            w = ring[b][:, 0:2, :].rearrange("p a (k f) -> p k a f", k=KC)
            for k in range(KC):
                g = k % 2
                last = TE.matmul(ps[64 * g:64 * g + 64, 2 + j, :], xtr[j][:, k, :], w[:, k, :, :],
                                 start=k < 2, stop=k >= KC - 2)
            last.then_inc(ml["s_up"][l], 1)

        def te_sum(l, e, j, first):
            TE.wait_ge(ml["s_upe"][l], e + 1)
            if not first:
                TE.wait_ge(ml["s_ac"][l], e - 1)
            for a2 in range(2):
                for f in range(FC):
                    src = upb[j][:, a2 * DE:(a2 + 1) * DE].rearrange("p (q f) -> p f q", f=FC)[:, f, :]
                    n = a2 * FC + f
                    last = TE.matmul(ps[:, 4 + j, n * CAP:(n + 1) * CAP], src, id2, start=True, stop=True)
            last.then_inc(ml["s_sm"][l], 1)

        def te_down(l, e, j, b, first):
            TE.wait_ge(ml["s_ac"][l], e + 1)
            if not first:
                TE.wait_ge(ml["s_ye"][l], e - 1)
                TE.wait_ge(ml["s_ye2"][l], e - 1)
            for f in range(FC):
                for nh in range(2):
                    last = TE.matmul(ps[64 * nh:64 * nh + 64, 6 + j, :], act_[j][:, f, :],
                                     ring[b][:, 2, f * D + nh * 512:f * D + (nh + 1) * 512],
                                     start=f == 0, stop=f == FC - 1)
            last.then_inc(ml["s_dn"][l], 1)

        def moe_tensor(l):
            te_xtrans(l, 0, 0, True)

            def four(i, first, last):
                for j in range(RING):
                    e = 4 * i + j
                    te_up(l, e, j % 2, j, 48 * (16 * l + i + 1), first and j < 2)
                    if not (last and j == 3):
                        te_xtrans(l, e + 1, (j + 1) % 2, first and j == 0)
                    if not (first and j == 0):
                        te_down(l, e - 1, (j + 1) % 2, (j - 1) % RING, first and j <= 2)
                    te_sum(l, e, j % 2, first and j < 2)
            four(0, True, False)
            with TE.Fori(1, 15) as i:
                four(i, False, False)
            four(15, False, True)
            te_down(l, 63, 1, 3, False)

        def moe_scalar(l):
            def one(e, j, first):
                S.wait_ge(ml["s_up"][l], e + 1)
                if not first:
                    S.wait_ge(ml["s_sm"][l], e - 1)
                S.activation(upb[j], ps[:, 2 + j, :], ACT.Copy).then_inc(ml["s_upe"][l], 1)
                S.wait_ge(ml["s_sm"][l], e + 1)
                if not first:
                    S.wait_ge(ml["s_ac"][l], e - 1)
                S.activation(sil[j], ps[:, 4 + j, 0:FC * CAP], ACT.Silu).then_inc(ml["s_si"][l], 1)

            def yout(e, j, first):
                S.wait_ge(ml["s_dn"][l], e + 1)
                if not first:
                    S.wait_ge(s_yst[l][j], 8 * (e - j))
                S.activation(yo[j][:, 512:1024], ps[CAP:2 * CAP, 6 + j, :], ACT.Copy).then_inc(ml["s_ye2"][l], 1)

            def four(i, first):
                for j in range(4):
                    e = 4 * i + j
                    if not (first and j == 0):
                        yout(e - 1, (j + 1) % 2, first and j <= 2)
                    one(e, j % 2, first and j < 2)
            four(0, True)
            with S.Fori(1, 16) as i:
                four(i, False)
            yout(63, 1, False)

        def moe_gpsimd(l):
            G.wait_ge(s_dst, l + 1)
            G.wait_ge(s_hst, 64 * l + 16 * TC)
            ex_gather(l, 0, 0, True)
            ex_gather(l, 1, 1, True)

            def four(i, first, last):
                for j in range(4):
                    e = 4 * i + j
                    if not (last and j >= 2):
                        ex_gather(l, e + 2, j % 2)
                    if not (first and j == 0):
                        ex_scatter(l, e - 1, (j + 1) % 2)
            four(0, True, False)
            with G.Fori(1, 15) as i:
                four(i, False, False)
            four(15, False, True)
            ex_scatter(l, 63, 1)

        def moe_vector(l):
            def xt(e, j, first):
                V.wait_ge(ml["s_xtp"][l], e + 1)
                if not first:
                    V.wait_ge(ml["s_up"][l], e - 1)
                V.tensor_copy(xtr[j].rearrange("p k s -> p (k s)"), ps[:, j, :]).then_inc(ml["s_xte"][l], 1)

            def act(e, j, first):
                V.wait_ge(ml["s_si"][l], e + 1)
                if not first:
                    V.wait_ge(ml["s_dn"][l], e - 1)
                V.tensor_tensor(act_[j].rearrange("p f s -> p (f s)"), sil[j], ps[:, 4 + j, FC * CAP:2 * FC * CAP],
                                ALU.mult).then_inc(ml["s_ac"][l], 1)

            def yout(e, j, first):
                V.wait_ge(ml["s_dn"][l], e + 1)
                if not first:
                    V.wait_ge(s_yst[l][j], 8 * (e - j))
                V.tensor_copy(yo[j][:, 0:512], ps[0:CAP, 6 + j, :]).then_inc(ml["s_ye"][l], 1)

            xt(0, 0, True)

            def four(i, first, last):
                for j in range(4):
                    e = 4 * i + j
                    if not (last and j == 3):
                        xt(e + 1, (j + 1) % 2, first and j == 0)
                    if not (first and j == 0):
                        yout(e - 1, (j + 1) % 2, first and j <= 2)
                    act(e, j % 2, first and j < 2)
            four(0, True, False)
            with V.Fori(1, 15) as i:
                four(i, False, False)
            four(15, False, True)
            yout(63, 1, False)

        def expert_weights(b, w, e, s):
            for n, (name, k) in enumerate((("moe_w1", KC), ("moe_w3", KC), ("moe_w2", FC))):
                src = a[name][w][bass.ds(e, 1), :, :].rearrange("a (p k) f -> p (a k f)", k=k)
                nc.sync.dma_start(ring[b][:, n, :], src).then_inc(s, 16)

        def moe_sync(l, ahead):
            SP = nc.sync
            for e in range(ahead, RING):
                expert_weights(e, l, e, s_ring[e])
            with SP.Fori(1, 16) as i:
                for j in range(RING):
                    SP.wait_ge(ml["s_dn"][l], 4 * i + j - 3)
                    SP.sem_inc(s_gate, 1)
                    expert_weights(j, l, 4 * i + j, s_ring[j])

        s_gate = sem("s_gate")

        OX, OXE, OUP, OUE, OSM, OSI, OAC, ODN, OYE, OYR = range(1, 11)
        STEPS = 10

        def extra_blocks(eng, l, body):
            eng.wait_ge(s_ov, l + 1)
            nov = eng.value_load(ovi[0:1, 15:16], min_val=0, max_val=OVMAX)
            with eng.If(0 < nov):
                with eng.Fori(0, OVMAX) as i:
                    with eng.If(i < nov):
                        body(i)

        def extra_tensor(l):
            def body(i):
                TE.wait_ge(ml["s_ox"][l], 16 * (i + 1))
                TE.sem_inc(s_gate4, 1)
                for k in range(KC):
                    last = TE.transpose(ps[:, 0, k * CAP:(k + 1) * CAP],
                                        xin[0][0:CAP, :].rearrange("p (q k) -> p k q", k=KC)[:, k, :],
                                        ident[0:CAP, 0:CAP])
                last.then_inc(ml["s_ostep"][l], 1)
                TE.wait_ge(ml["s_ostep"][l], STEPS * i + OXE)
                TE.wait_ge(ml["s_ow"][l], 48 * (i + 1))
                w = ring[0][:, 0:2, :].rearrange("p a (k f) -> p k a f", k=KC)
                for k in range(KC):
                    g = k % 2
                    last = TE.matmul(ps[64 * g:64 * g + 64, 2, :], xtr[0][:, k, :], w[:, k, :, :],
                                     start=k < 2, stop=k >= KC - 2)
                last.then_inc(ml["s_ostep"][l], 1)
                TE.wait_ge(ml["s_ostep"][l], STEPS * i + OUE)
                for n in range(2 * FC):
                    a2, f = n // FC, n % FC
                    src = upb[0][:, a2 * DE:(a2 + 1) * DE].rearrange("p (q f) -> p f q", f=FC)[:, f, :]
                    last = TE.matmul(ps[:, 4, n * CAP:(n + 1) * CAP], src, id2, start=True, stop=True)
                last.then_inc(ml["s_ostep"][l], 1)
                TE.wait_ge(ml["s_ostep"][l], STEPS * i + OAC)
                for f in range(FC):
                    for nh in range(2):
                        last = TE.matmul(ps[64 * nh:64 * nh + 64, 6, :], act_[0][:, f, :],
                                         ring[0][:, 2, f * D + nh * 512:f * D + (nh + 1) * 512],
                                         start=f == 0, stop=f == FC - 1)
                last.then_inc(ml["s_ostep"][l], 1)
            extra_blocks(TE, l, body)

        def extra_scalar(l):
            def body(i):
                S.wait_ge(ml["s_ostep"][l], STEPS * i + OUP)
                S.activation(upb[0], ps[:, 2, :], ACT.Copy).then_inc(ml["s_ostep"][l], 1)
                S.wait_ge(ml["s_ostep"][l], STEPS * i + OSM)
                S.activation(sil[0], ps[:, 4, 0:FC * CAP], ACT.Silu).then_inc(ml["s_ostep"][l], 1)
                S.wait_ge(ml["s_ostep"][l], STEPS * i + OYE)
                S.activation(yo[0][:, 512:1024], ps[CAP:2 * CAP, 6, :], ACT.Copy).then_inc(ml["s_ostep"][l], 1)
            extra_blocks(S, l, body)

        def extra_vector(l):
            def body(i):
                V.wait_ge(ml["s_ostep"][l], STEPS * i + OX)
                V.tensor_copy(xtr[0].rearrange("p k s -> p (k s)"), ps[:, 0, :]).then_inc(ml["s_ostep"][l], 1)
                V.wait_ge(ml["s_ostep"][l], STEPS * i + OSI)
                V.tensor_tensor(act_[0].rearrange("p f s -> p (f s)"), sil[0], ps[:, 4, FC * CAP:2 * FC * CAP],
                                ALU.mult).then_inc(ml["s_ostep"][l], 1)
                V.wait_ge(ml["s_ostep"][l], STEPS * i + ODN)
                V.tensor_copy(yo[0][:, 0:512], ps[0:CAP, 6, :]).then_inc(ml["s_ostep"][l], 1)
            extra_blocks(V, l, body)

        def extra_gpsimd(l):
            def body(i):
                glink_at(G.tensor_copy(icol[0:CAP, 0:1], blkidx[0:CAP, 0, bass.ds(i + NE, 1)]), s_oic[l], 2 * i + 1)
                G.indirect_dma_start(xin[0][0:CAP, :], None, hrow[l],
                                     bass.IndirectOffsetOnAxis(ap=icol[0:CAP, 0:1], axis=0),
                                     bounds_check=T - 1, oob_is_err=False).then_inc(ml["s_ox"][l], 16)
                G.wait_ge(ml["s_ostep"][l], STEPS * i + OYR)
                glink_at(G.tensor_copy(icol[0:CAP, 2:3], blkidx[0:CAP, 1, bass.ds(i + NE, 1)]), s_oic[l], 2 * i + 2)
                G.indirect_dma_start(ytok[l], bass.IndirectOffsetOnAxis(ap=icol[0:CAP, 2:3], axis=0),
                                     yo[0], None, bounds_check=2 * T - 1, oob_is_err=False)\
                    .then_inc(ml["s_oys"][l], 16)
                G.wait_ge(ml["s_oys"][l], 16 * (i + 1))
                G.sem_inc(s_gate2, 1)
            extra_blocks(G, l, body)

        s_gate2, s_gate4 = sem("s_gate2"), sem("s_gate4")
        s_ic = [[sem(f"s_ic{l}{j}") for j in range(2)] for l in range(2)]
        s_oic = [sem(f"s_oic{l}") for l in range(2)]

        def extra_sync(l):
            SP = nc.sync
            SP.wait_ge(s_ov, l + 1)
            SP.wait_ge(ml["s_dn"][l], NE)

            nov = SP.value_load(ovi[0:1, 15:16], min_val=0, max_val=OVMAX)
            with SP.If(0 < nov):
                with SP.Fori(0, OVMAX) as i:
                    with SP.If(i < nov):
                        e = SP.value_load(ovi[0:1, bass.ds(i, 1)], min_val=0, max_val=NE - 1)
                        expert_weights(0, l, e, ml["s_ow"][l])
                        SP.wait_ge(ml["s_oys"][l], 16 * (i + 1))
                        SP.sem_inc(s_gate, 1)


        def combine_sync(l):
            for j in range(2):
                nc.sync.wait_ge(s_yst[l][j], 8 * NE)
            for n in range(8):
                c, k = n // 2, n % 2
                if n >= 4:
                    nc.sync.wait_ge(ml["s_ga"][l], n - 3)
                nc.sync.dma_start(gath[:, n % 4, :], ytok[l][k * T + c * P:k * T + (c + 1) * P, :])\
                    .then_inc(s_gat[n % 4], 16)

        s_gat = [sem(f"s_gat{i}") for i in range(4)]

        def combine_vector(l):
            for n in range(8):
                c, k = n // 2, n % 2
                V.wait_ge(s_gat[n % 4], 16 * (2 * l + n // 4 + 1))
                ins = V.scalar_tensor_tensor(x[:, c, :], gath[:, n % 4, :], g12[:, 4 * k + c:4 * k + c + 1],
                                             x[:, c, :], ALU.mult, ALU.add)
                ins.then_inc(ml["s_ga"][l], 1)
                V.wait_ge(ml["s_ga"][l], n + 1)

        PARAMS = [("p_s5", s5p), ("p_ch", chp), ("p_bre", bre), ("p_bim", bim)]
        NPAR = len(PARAMS) + 4

        block = ctx.enter_context(nc.Block())

        @block.sync
        def _(sp):
            for c in range(TC):
                sp.dma_start(x[:, c, :], a["x"][c * P:(c + 1) * P, :]).then_inc(s_x[c], 16)
            sp.dma_start(con[:, :], a["p_const"]).then_inc(s_con, 16)
            wv = a["ev_w_in"].rearrange("(p k) n -> p k n", k=KC)
            for n, j in enumerate((1, 0)):
                if n:
                    sp.wait_ge(s_par, 16 * NPAR)
                sp.dma_start(wcol[n], wv[:, :, j * 512:(j + 1) * 512]).then_inc(s_ev_x[n], 16)
            sp.wait_ge(s_pj, 4)
            sp.dma_start(wcol[0], wv[:, :, 1024:1536]).then_inc(s_ev_x[2], 16)
            wo = a["ev_w_out"].rearrange("(k p) n -> p k n", p=P)
            sp.wait_ge(s_pj, 12)
            for n in range(2):
                sp.dma_start(wout[n], wo[:, :, n * 512:(n + 1) * 512]).then_inc(s_wb[n], 16)
            sp.wait_ge(s_st, NS5)
            expert_weights(0, 0, 0, s_ring[0])
            expert_weights(1, 0, 1, s_ring[1])
            sp.wait_ge(s_bar, 4)
            expert_weights(2, 0, 2, s_ring[2])
            expert_weights(3, 0, 3, s_ring[3])
            wv = a["mla_w_in"].rearrange("(p k) n -> p k n", k=KC)
            for n in range(2):
                sp.dma_start(win[n], wv[:, :, n * HW:(n + 1) * HW]).then_inc(s_win, 16)
            moe_sync(0, 4)
            extra_sync(0)
            combine_sync(0)
            sp.wait_ge(s_ch, TC)
            sp.dma_start(wuq, a["mla_w_uq"].rearrange("(k p) n -> p k n", p=P)).then_inc(s_uq, 16)
            sp.wait_ge(s_c, TC)
            sp.dma_start(wukv, a["mla_w_ukv"].rearrange("(k p) n -> p k n", p=P)).then_inc(s_ukv, 16)
            sp.wait_ge(s_q, unit("kv", TC - 1, 3) + 1)
            wo = a["mla_w_o"].rearrange("(k p) n -> p k n", p=P)
            for n in range(2):
                sp.dma_start(wout[n], wo[:, :, n * 512:(n + 1) * 512]).then_inc(s_wb[n], 16)
            sp.wait_ge(s_sc, H * TC)
            for e in range(3):
                expert_weights(e, 1, e, s_ring[e])
            sp.wait_ge(s_bar, 12)
            moe_sync(1, 3)
            extra_sync(1)
            combine_sync(1)
            sp.wait_ge(s_out, 16 * TC)
            for l in range(2):
                for j in range(2):
                    sp.wait_ge(s_yst[l][j], 8 * NE)

        @block.gpsimd
        def _(g):
            def row_gain(n):
                if n:
                    g.wait_ge(s_h, TC * n)
                g.dma_start(gain[:, :], a["p_norms"][n:n + 1, :].to_broadcast([P, D])).then_inc(s_gain, 16)

            def router(l):
                src = a["moe_w_group"][l].rearrange("(p k) n -> p k n", k=KC)
                g.dma_start(rwb[:, :, 0:8], src).then_inc(s_rw, 16)
                src = a["moe_w_expert"][l].rearrange("(p k) n -> p k n", k=KC)
                g.dma_start(rwb[:, :, 8:72], src).then_inc(s_rw, 16)
                g.dma_start(rbias[:, :], a["p_rbias"][l:l + 1, :].to_broadcast([P, 72])).then_inc(s_rw, 16)

            row_gain(0)
            for name, dst_ in PARAMS:
                g.dma_start(dst_, a[name]).then_inc(s_par, 16)
            glink(g.memset(cmat, 0.0))
            for j in range(2):
                for q in range(2):
                    r = slice(64 * q, 64 * q + 64)
                    g.dma_start(cmat[r, j, :, 16 * q:16 * q + 16], a["p_c"][j, r, :, :]).then_inc(s_par, 16)
            g.wait_ge(s_tr, TC)
            g.dma_start(lruw, a["p_gate_w"]).then_inc(s_lw, 16)
            g.wait_ge(s_ssq, TC)
            g.dma_start(glu, a["p_glu_w"]).then_inc(s_lw, 16)
            router(0)
            even_gpsimd()
            g.wait_ge(s_bu, NS5)
            row_gain(1)
            barrier(g, 1)
            for l in range(2):
                if l == 0:
                    g.wait_ge(s_h, 2 * TC)
                    row_gain(2)
                    g.dma_start(posi[:, :], a["p_pos"]).then_inc(s_pos, 16)
                    for d_, nm in ((gnq, "p_gnq"), (gnk, "p_gnk"), (gc5, "p_gc5")):
                        g.dma_start(d_, a[nm]).then_inc(s_pos2, 16)
                    for d_, nm in ((grq, "p_grq"), (grk, "p_grk")):
                        g.dma_start(d_, a[nm].to_broadcast([P, ROPE])).then_inc(s_pos2, 16)
                moe_gpsimd(l)
                for j in range(2):
                    g.wait_ge(s_yst[l][j], 8 * NE)
                extra_gpsimd(l)
                barrier(g, 2 + 2 * l)
                if l == 0:
                    router(1)
                    g.wait_ge(s_qn, TC)
                    row_gain(3)
                    barrier(g, 3)

        @block.scalar
        def _(act):
            act.wait_ge(s_eps, 1)
            norm_sums(0)
            norm_scalar(0)
            even_scalar()
            norm_sums(1)
            barrier(act, 1)
            for l in range(2):
                norm_scalar(1 + 2 * l)
                for c in range(TC):
                    act.wait_ge(s_h, TC * (2 * l + 1) + c + 1)
                    act.dma_start(hrow[l][c * P:(c + 1) * P, :], h[:, c, :]).then_inc(s_hst, 16)
                route_scalar(l)
                moe_scalar(l)
                for j in range(2):
                    act.wait_ge(s_yst[l][j], 8 * NE)
                extra_scalar(l)
                if l:
                    for c in range(TC):
                        act.wait_ge(ml["s_ga"][1], 2 * c + 2)
                        act.dma_start(out[c * P:(c + 1) * P, :], x[:, c, :]).then_inc(s_out, 16)
                else:
                    norm_sums(2)
                barrier(act, 2 + 2 * l)
                if l == 0:
                    norm_scalar(2)
                    act.wait_ge(s_pos2, 80)
                    odd_scalar()
                    norm_sums(3)
                    barrier(act, 3)

        @block.vector
        def _(v):
            v.memset(eps, EPS)
            vlink(v.memset(halfpi, math.pi / 2))
            v.nop().then_inc(s_eps, 1)
            for c in range(TC):
                norm_rows(0, c)
            v.wait_ge(s_con, 16)
            norm_vector(0)
            even_vector()
            barrier(v, 1)
            for l in range(2):
                norm_vector(1 + 2 * l)
                route_vector(l)
                moe_vector(l)
                for j in range(2):
                    v.wait_ge(s_yst[l][j], 8 * NE)
                extra_vector(l)
                combine_vector(l)
                if l == 0:
                    for c in range(TC):
                        norm_rows(2, c)
                barrier(v, 2 + 2 * l)
                if l == 0:
                    norm_vector(2)
                    v.wait_ge(s_pos2, 80)
                    odd_vector()
                    barrier(v, 3)

        @block.tensor
        def _(t):
            t.wait_ge(s_con, 16)
            norm_tensor(0)
            t.wait_ge(s_par, 16 * NPAR)
            even_tensor()
            barrier(t, 1)
            for l in range(2):
                norm_tensor(1 + 2 * l)
                route_tensor(l)
                table_tensor(l)
                moe_tensor(l)
                extra_tensor(l)
                barrier(t, 2 + 2 * l)
                if l == 0:
                    norm_tensor(2)
                    odd_tensor()
                    barrier(t, 3)


def kernel(**inputs):
    import concourse.bacc as _bacc
    from concourse.bass_utils import run_bass_kernel_spmd as _run

    g = {n: np.asarray(v) for n, v in inputs.items()}

    def states(v):
        v = v.reshape((NS5, 2, 64) + v.shape[2:])
        return np.moveaxis(v, 0, 2).reshape((P, NS5) + v.shape[3:])

    def channels(v):
        return v.reshape(MT, P).T

    ldt = np.broadcast_to(g["s5_log_dt"][0][:, None], (32, 64))
    arr = {
        "x": g["x"].reshape(T, D),
        "ev_w_in": g["ev_w_in"][0], "ev_w_out": g["ev_w_out"][0],
        "mla_w_in": g["mla_w_in"][0], "mla_w_uq": g["mla_w_uq"][0],
        "mla_w_ukv": g["mla_w_ukv"][0], "mla_w_o": g["mla_w_o"][0],
        "moe_w_group": g["moe_w_group"], "moe_w_expert": g["moe_w_expert"],
        "moe_w1": g["moe_w1"], "moe_w3": g["moe_w3"], "moe_w2": g["moe_w2"],
        "p_const": shape_constants(),
        "p_norms": np.stack([g["ev_norm"][0], g["ffn_norm"][0], g["od_norm"][0], g["ffn_norm"][1]]),
        "p_rbias": np.concatenate([g["moe_b_group"], g["moe_b_expert"]], axis=1),
        "p_s5": np.concatenate([states(g["s5_lambda_re"][0]), states(g["s5_lambda_im"][0]), states(ldt)], axis=1),
        "p_ch": np.concatenate([channels(g[n][0].reshape(-1)) for n in
                                ("s5_d", "s5_glu_b", "lru_conv_b", "lru_ba", "lru_bi", "lru_lambda")]
                               + [channels(g["lru_conv_w"][0][k]) for k in range(4)], axis=1),
        "p_bre": states(g["s5_b_re"][0]), "p_bim": states(g["s5_b_im"][0]),
        "p_c": np.stack([states(g[n][0].transpose(0, 2, 1)) for n in ("s5_c_re", "s5_c_im")]),
        "p_gate_w": np.stack([g[n][0].reshape(MT, P, 64).transpose(1, 0, 2) for n in ("lru_wa", "lru_wi")], axis=1),
        "p_glu_w": g["s5_glu_w"][0].reshape(MT, P, W5).transpose(1, 0, 2),
        "p_pos": g["positions"].reshape(TC, P).T,
        "p_gnq": g["mla_q_norm"][0][:NOPE].reshape(P, 1), "p_gnk": g["mla_k_norm"][0][:NOPE].reshape(P, 1),
        "p_grq": g["mla_q_norm"][0][NOPE:].reshape(1, ROPE), "p_grk": g["mla_k_norm"][0][NOPE:].reshape(1, ROPE),
        "p_gc5": np.concatenate([g["mla_cq_norm"][0], g["mla_ckv_norm"][0]]).reshape(5, P).T,
    }
    nc = _bacc.Bacc("TRN2", target_bir_lowering=False, num_devices=1)
    arrays, aps = {}, {}
    for name, v in arr.items():
        v = np.ascontiguousarray(v)
        arrays[f"in_{name}"] = v
        aps[name] = nc.dram_tensor(f"in_{name}", v.shape, mybir.dt.from_np(v.dtype), kind="ExternalInput").ap()
    out = nc.dram_tensor("out_0", (T, D), F32, kind="ExternalOutput").ap()
    hybrid_decoder(nc, aps, out)
    r = _run(nc, [arrays], core_ids=[0])
    return r.results[0]["out_0"].reshape(1, T, D)
```
